# Optimizing a Trainium2 kernel written in Bass

```python
import jax, jax.numpy as jnp
from jax import lax
import numpy as np

D_MODEL = 1024
BATCH = 1
SEQ = 512
DEPTH = 2

ATT_WIDTH = D_MODEL // 2
ATT_HEADS = 8
HEAD_DIM = ATT_WIDTH // ATT_HEADS
Q_BLOCK = 128
GMLP_WIDTH = D_MODEL // 4
GMLP_GROUPS = 4
GMLP_GROUP_DIM = GMLP_WIDTH // GMLP_GROUPS
CHUNK = 128
CONV_WIDTH = D_MODEL // 4
CONV_GROUPS = 4
CONV_K = 3
MIX_WIDTH = ATT_WIDTH + GMLP_WIDTH + CONV_WIDTH
SPLIT_SIZES = (ATT_WIDTH, ATT_WIDTH, ATT_WIDTH, ATT_HEADS,
               GMLP_WIDTH, GMLP_WIDTH,
               CONV_WIDTH, CONV_WIDTH, CONV_WIDTH)
IN_COLS = sum(SPLIT_SIZES)

PEER_HEADS = 8
N_KEYS = 128
N_EXPERTS = N_KEYS * N_KEYS
PEER_TOPK = 16
D_KEY = 256
D_HALF = D_KEY // 2
PEER_CHUNK = 128

EPS = 1e-6

kernel_name = "hybrid_fox_gmlp_conv_peer"

def rmsnorm(x, g):
    x32 = x.astype(jnp.float32)
    y = x32 * lax.rsqrt(jnp.mean(x32 * x32, axis=-1, keepdims=True) + EPS)
    return (y * g.astype(jnp.float32)).astype(x.dtype)

def forgetting_attention(q, k, v, cum_logf):
    Bn, S, H, dh = q.shape
    nq = S // Q_BLOCK
    scale = dh ** -0.5
    kh = k.transpose(0, 2, 1, 3)
    vh = v.transpose(0, 2, 1, 3)
    Fk = cum_logf.transpose(0, 2, 1)
    qb = q.reshape(Bn, nq, Q_BLOCK, H, dh).transpose(1, 0, 3, 2, 4)
    Fq = Fk.reshape(Bn, H, nq, Q_BLOCK).transpose(2, 0, 1, 3)
    key_pos = jnp.arange(S)

    def block(args):
        q_blk, fq_blk, i = args
        q_pos = i * Q_BLOCK + jnp.arange(Q_BLOCK)
        logits = jnp.einsum('bhqd,bhkd->bhqk', q_blk, kh).astype(jnp.float32) * scale
        logits = logits + fq_blk[..., :, None] - Fk[..., None, :]
        mask = key_pos[None, :] <= q_pos[:, None]
        logits = jnp.where(mask, logits, -1e30)
        p = jax.nn.softmax(logits, axis=-1).astype(vh.dtype)
        return jnp.einsum('bhqk,bhkd->bhqd', p, vh)

    out = lax.map(block, (qb, Fq, jnp.arange(nq)))
    return out.transpose(1, 0, 3, 2, 4).reshape(Bn, S, H * dh)

def chunked_gmlp(zu, zv, sgu_g, w_spatial, b_spatial):
    Bn, S, _ = zu.shape
    u = jax.nn.gelu(zu)
    v = jax.nn.gelu(zv).reshape(Bn, S, GMLP_GROUPS, GMLP_GROUP_DIM)
    v = rmsnorm(v, sgu_g.reshape(GMLP_GROUPS, GMLP_GROUP_DIM))
    v = v.reshape(Bn, S // CHUNK, CHUNK, GMLP_GROUPS, GMLP_GROUP_DIM)
    tril = jnp.tril(jnp.ones((CHUNK, CHUNK), dtype=bool))
    w = jnp.where(tril[None], w_spatial, jnp.zeros_like(w_spatial))
    mixed = jnp.einsum('gts,bcsgd->bctgd', w, v) + b_spatial.T[:, :, None]
    return u * mixed.reshape(Bn, S, GMLP_WIDTH)

def causal_shift(x, n):
    return jnp.pad(x, ((0, 0), (n, 0), (0, 0)))[:, :x.shape[1], :]

def short_gated_conv(h_in, gate_b, gate_c, conv_w):
    z = gate_c * h_in
    y = conv_w[0] * causal_shift(z, 2) + conv_w[1] * causal_shift(z, 1) + conv_w[2] * z
    return gate_b * y

def peer_ffn(h, w_query, sub_keys, expert_u, expert_v):
    Bn, S, D = h.shape
    T = Bn * S
    ht = h.reshape(T, D)
    q = (ht @ w_query).reshape(T, PEER_HEADS, D_KEY)
    s1 = jnp.einsum('thd,kd->thk', q[..., :D_HALF], sub_keys[0]).astype(jnp.float32)
    s2 = jnp.einsum('thd,kd->thk', q[..., D_HALF:], sub_keys[1]).astype(jnp.float32)
    v1, i1 = lax.top_k(s1, PEER_TOPK)
    v2, i2 = lax.top_k(s2, PEER_TOPK)
    cand = (v1[..., :, None] + v2[..., None, :]).reshape(T, PEER_HEADS, PEER_TOPK * PEER_TOPK)
    sc, ci = lax.top_k(cand, PEER_TOPK)
    e_idx = (jnp.take_along_axis(i1, ci // PEER_TOPK, axis=-1) * N_KEYS
             + jnp.take_along_axis(i2, ci % PEER_TOPK, axis=-1))
    gate = jax.nn.softmax(sc, axis=-1).astype(h.dtype)
    nc = T // PEER_CHUNK

    def chunk(args):
        xc, ec, gc = args
        a = jnp.einsum('chkd,cd->chk', expert_u[ec], xc)
        w = jax.nn.gelu(a) * gc
        return jnp.einsum('chk,chkd->cd', w, expert_v[ec])

    out = lax.map(chunk, (ht.reshape(nc, PEER_CHUNK, D),
                          e_idx.reshape(nc, PEER_CHUNK, PEER_HEADS, PEER_TOPK),
                          gate.reshape(nc, PEER_CHUNK, PEER_HEADS, PEER_TOPK)))
    return out.reshape(Bn, S, D)

def setup_inputs(seed: int = 0) -> dict:
    key = jax.random.key(seed)
    ks = jax.random.split(key, 16)
    f32 = jnp.float32
    nrm = lambda k, shp: jax.random.normal(k, shp, dtype=f32)
    return {
        "x": nrm(ks[0], (BATCH, SEQ, D_MODEL)),
        "norm1_g": 1.0 + 0.05 * nrm(ks[1], (DEPTH, D_MODEL)),
        "w_in": nrm(ks[2], (DEPTH, D_MODEL, IN_COLS)) * D_MODEL ** -0.5,
        "b_forget": 3.0 + 0.5 * nrm(ks[3], (DEPTH, ATT_HEADS)),
        "sgu_norm_g": 1.0 + 0.05 * nrm(ks[4], (DEPTH, GMLP_WIDTH)),
        "w_spatial": nrm(ks[5], (DEPTH, GMLP_GROUPS, CHUNK, CHUNK)) * CHUNK ** -0.5,
        "b_spatial": 1.0 + 0.1 * nrm(ks[6], (DEPTH, GMLP_GROUPS, CHUNK)),
        "conv_w": nrm(ks[7], (DEPTH, CONV_K, CONV_WIDTH)) * CONV_K ** -0.5,
        "mix_norm_g": 1.0 + 0.05 * nrm(ks[8], (DEPTH, MIX_WIDTH)),
        "w_out": nrm(ks[9], (DEPTH, MIX_WIDTH, D_MODEL)) * MIX_WIDTH ** -0.5,
        "norm2_g": 1.0 + 0.05 * nrm(ks[10], (DEPTH, D_MODEL)),
        "w_query": nrm(ks[11], (DEPTH, D_MODEL, PEER_HEADS * D_KEY)) * D_MODEL ** -0.5,
        "sub_keys": nrm(ks[12], (DEPTH, 2, N_KEYS, D_HALF)) * D_HALF ** -0.5,
        "expert_u": nrm(ks[13], (DEPTH, N_EXPERTS, D_MODEL)) * D_MODEL ** -0.5,
        "expert_v": nrm(ks[14], (DEPTH, N_EXPERTS, D_MODEL)) * PEER_HEADS ** -0.5,
        "final_g": 1.0 + 0.05 * nrm(ks[15], (D_MODEL,)),
    }

def reference(x, norm1_g, w_in, b_forget, sgu_norm_g, w_spatial, b_spatial, conv_w,
              mix_norm_g, w_out, norm2_g, w_query, sub_keys, expert_u, expert_v, final_g):
    Bn, S, _ = x.shape
    split_at = [int(s) for s in np.cumsum(SPLIT_SIZES)[:-1]]
    for l in range(DEPTH):
        h = rmsnorm(x, norm1_g[l])
        z = h @ w_in[l]
        zq, zk, zv, zf, gu, gv, c_in, c_b, c_c = jnp.split(z, split_at, axis=-1)
        logf = jax.nn.log_sigmoid((zf + b_forget[l]).astype(jnp.float32))
        cum_logf = jnp.cumsum(logf, axis=1)
        shp = (Bn, S, ATT_HEADS, HEAD_DIM)
        o_att = forgetting_attention(zq.reshape(shp), zk.reshape(shp), zv.reshape(shp), cum_logf)
        o_gmlp = chunked_gmlp(gu, gv, sgu_norm_g[l], w_spatial[l], b_spatial[l])
        o_conv = short_gated_conv(c_in, c_b, c_c, conv_w[l])
        g = mix_norm_g[l]
        mixed = jnp.concatenate([
            rmsnorm(o_att, g[:ATT_WIDTH]),
            rmsnorm(o_gmlp, g[ATT_WIDTH:ATT_WIDTH + GMLP_WIDTH]),
            rmsnorm(o_conv, g[ATT_WIDTH + GMLP_WIDTH:]),
        ], axis=-1)
        x = x + mixed @ w_out[l]
        h2 = rmsnorm(x, norm2_g[l])
        x = x + peer_ffn(h2, w_query[l], sub_keys[l], expert_u[l], expert_v[l])
    return rmsnorm(x, final_g)


_drawn_inputs = setup_inputs


def setup_inputs(seed=0):
    import zlib

    import numpy as np

    out = dict(_drawn_inputs(seed))
    spreads = {}
    factors = {}
    for name, (base, spread) in spreads.items():
        noise = np.random.default_rng([zlib.crc32(name.encode()), seed]).standard_normal(out[name].shape)
        drawn = base * np.exp(spread * noise) if base else spread * noise
        out[name] = __import__('jax').numpy.asarray(drawn.astype(out[name].dtype))
    for name, factor in factors.items():
        out[name] = (out[name] * factor).astype(out[name].dtype)
    return out
```

```python
from contextlib import ExitStack

import concourse.bass as bass
from concourse import mybir

ALU = mybir.AluOpType
ACT = mybir.ActivationFunctionType
AX = mybir.AxisListType
F32 = mybir.dt.float32
BF16 = mybir.dt.bfloat16
U32 = mybir.dt.uint32

P = 128
EPS = 1e-6
NEG = -3.0e38
MASKED = -1e30
SLAB = 512
NSLAB = 3
RING = 6
T_LAG, V_LAG, O_LAG, AT_LAG = 2, 3, 4, 5
DEEP = 3
NBUF = 8
GROUP = 2
BODY = 8
PARTS = 8


def trunk_kernel(nc, x_d, norm1_g, w_in, b_forget, sgu_g, w_spatial, b_spatial, conv_w, mix_g, w_out,
                 norm2_g, w_query, sub_keys, uv, final_g, out_d):
    L = norm1_g.shape[0]
    T, D = x_d.shape
    TILES = T // P
    DC = D // P
    H = b_forget.shape[1]
    AW = D // 2
    DH = AW // H
    GW = sgu_g.shape[1]
    GG = w_spatial.shape[2]
    GD = GW // GG
    CW = conv_w.shape[3] * P
    CC = CW // P
    AC = AW // P
    GC = GW // P
    KEYS = sub_keys.shape[3]
    NE = uv.shape[0] // L
    PH = w_query.shape[3] // 2 // P
    UNITS = 2 * PH
    K = 16
    SLOTS = PH * K
    HC = PH // 2
    CS = HC * K
    SCALE = float(DH) ** -0.5
    NQ = UNITS // (SLAB // P)
    LOOP = SLOTS // PARTS // BODY
    IN_COLS = w_in.shape[3]
    O_Q, O_K, O_V = 0, AW, 2 * AW
    O_F = 3 * AW
    O_G = O_F + H
    O_C = O_G + 2 * GW
    in_slabs = [(O_F, H, 0), (O_C + 2 * CW, CW, H), (O_C, 2 * CW, None), (O_G, 2 * GW, None),
                (O_V, AW, None), (O_Q, AW, None), (O_K, AW, None)]
    N_IN = 6
    N_OUT = D // SLAB
    SLABS = N_IN + N_OUT + NQ
    S_F, S_C, S_G, S_V, S_Q, S_K, S_O = 0, 1, 2, 3, 4, 5, 6
    S_QY = S_O + N_OUT

    UN = TILES * H
    order = [("T1", i, f) for i in range(TILES) for f in range(2)]
    order += [("ZF",)] + [(n, c) for n in ("CC", "CI", "CB") for c in range(CC)]
    order += [("G", i) for i in range(TILES)] + [("V", i) for i in range(TILES)]
    order += [("Q", c) for c in range(AC)] + [("K", c) for c in range(AC)]
    order += [("FB", h) for h in range(H)] + [("GM", i) for i in range(TILES)] + [("CS",)]
    order += [("GT", i) for i in range(TILES)]
    for s in range(UN + AT_LAG):
        order += [("S", s)] if s < UN else []
        order += [("P", s - T_LAG)] if T_LAG <= s < UN + T_LAG else []
        order += [("AT", (s - AT_LAG) // H)] if s >= AT_LAG and (s - AT_LAG) % H == H - 1 else []
    order += [(n, f, i) for f in range(N_OUT) for i in range(TILES) for n in ("OA", "OG", "OC")]
    order += [("T2", i, f) for i in range(TILES) for f in range(2)]
    for c in range(UNITS):
        order += [("QY", c)] + ([("SC", c - 1)] if c else [])
    order += [("SC", UNITS - 1)]
    place = {key: n for n, key in enumerate(order)}
    PER = len(order)

    def turn(l, *key):
        return l * PER + place[key]

    ctx = ExitStack()
    with ctx:
        def sb(name, shape, dt=F32):
            return ctx.enter_context(nc.sbuf_tensor(name, shape, dt))

        def sem(name):
            return ctx.enter_context(nc.semaphore(name))

        banks = [ctx.enter_context(nc.psum_tensor(f"bank{n}", [P, 512], F32)) for n in range(8)]

        x = sb("x", [P, TILES, D])
        h_nat = sb("h_nat", [P, TILES, D])
        wide = sb("wide", [P, DC, T])
        arena = sb("arena", [P, NBUF, 2 * D])
        slabs = [sb(f"slab{n}", [P, DC * SLAB]) for n in range(NSLAB)]
        scores = sb("scores", [P, TILES, UNITS, KEYS])
        gain = sb("gain", [P, D])
        diag = sb("diag", [P, NBUF, P])
        ident = sb("ident", [P, P])
        ident16 = sb("ident16", [P, P], BF16)
        causal = sb("causal", [P, P], BF16)
        zero16 = sb("zero16", [P, P], BF16)
        bsp = sb("bsp", [P, GG])
        mixg = sb("mixg", [P, DC])
        cw = sb("cw", [P, 3, CC])
        bf = sb("bf", [H, 1])
        ones = sb("ones", [P, 2])
        keysT = sb("keysT", [P, 2, KEYS])
        iota = sb("iota", [P, K])
        gate = sb("gate", [P, 2, SLOTS])
        eidx = sb("eidx", [P, 2, SLOTS], U32)
        stage = sb("stage", [P, NBUF], U32)
        gstage = sb("gstage", [P, BODY])
        dots = sb("dots", [P, BODY])
        gelu = sb("gelu", [P, BODY])
        wts = sb("wts", [P, BODY])
        stat = sb("stat", [P, 96])
        neghalf = sb("neghalf", [P, 16])

        flat = arena[:].rearrange("p a b -> p (a b)")

        def cut(region, at, shape):
            n = 1
            for s in shape:
                n *= s
            v = region[:, at:at + n]
            if len(shape) == 2:
                v = v.rearrange("p (a b) -> p a b", a=shape[0])
            return v, at + n

        at = 0
        qT, at = cut(flat, at, [AC, T])
        kT, at = cut(flat, at, [AC, T])
        v_nat, at = cut(flat, at, [TILES, AW])
        negF, at = cut(flat, at, [H, T])
        mixT, at = cut(flat, at, [DC, T])
        ug, at = cut(flat, at, [TILES, 2 * GW])
        qyT, _ = cut(gain[:], 0, [2, T])
        sflat = scores[:].rearrange("p a b c -> p (a b c)")
        at = 0
        logit, at = cut(sflat, at, [DEEP, T])
        prob, at = cut(sflat, at, [DEEP, T])
        probT, at = cut(sflat, at, [2, T])
        o_att, at = cut(sflat, at, [2, AW])
        at = 0
        zpad, at = cut(sflat, at, [CC, T + 2])
        y_cv, at = cut(sflat, at, [CC, T])
        c_c, at = cut(sflat, at, [CC, T])
        vn, at = cut(sflat, at, [TILES, GW])
        zf, at = cut(sflat, at, [4, T])
        sgu_b, at = cut(sflat, at, [GW])
        wsp, at = cut(sflat, at, [GG, P])
        assert at <= TILES * UNITS * KEYS, at
        wflat = wide[:].rearrange("p a b -> p (a b)")
        class Scratch:

            def __init__(self, region, at):
                self.cand, at = cut(region, at, [K * K])
                self.onehot, at = cut(region, at, [CS * K])
                self.vals, at = cut(region, at, [2 * HC, K])
                kidx, at = cut(region, at, [2 * HC, K])
                self.top, at = cut(region, at, [HC, K])
                tidx, at = cut(region, at, [HC, K])
                tsel, at = cut(region, at, [CS])
                self.tself, at = cut(region, at, [CS])
                self.epart, at = cut(region, at, [2, CS])
                assert at <= region.shape[1]
                self.kidx, self.tidx, self.tsel = kidx.bitcast(U32), tidx.bitcast(U32), tsel.bitcast(U32)

        first_scratch, later_scratch = Scratch(flat, 2 * AC * T), Scratch(wflat, 0)

        def scratch(t, c):
            return later_scratch if t or c else first_scratch

        def chunk_no(l, t, c):
            return 2 * (l * TILES + t) + c

        junk = wflat[:, 0:D]
        ss, ms, rstd = stat[:, 0:4], stat[:, 4:8], stat[:, 8:12]
        ssm = stat[:, 12:24]
        rm = stat[:, 24:36]
        rmax, nmax = stat[:, 84:87], stat[:, 87:90]
        rsum, rinv = stat[:, 90:93], stat[:, 93:96]
        gs, gr = stat[:, 44:60], stat[:, 60:76]
        dn = stat[:, 76:84]

        s_const = sem("const_loaded")
        s_layer = sem("layer_const_loaded")
        s_gain = sem("gain_loaded")
        s_setup = sem("setup_done")
        s_slab = [sem(f"slab{n}_loaded") for n in range(NSLAB)]
        full = [sem(f"bank{n}_full") for n in range(RING)]
        free = [sem(f"bank{n}_free") for n in range(RING)]
        s_vec = sem("vector_step")
        s_act = sem("scalar_step")
        s_sq = sem("square_summed")
        s_ms = sem("mean_square_ready")
        s_rms = sem("inverse_rms_ready")
        s_h = sem("h_ready")
        s_sp = sem("softplus_ready")
        s_zf = sem("forget_logit_ready")
        s_F = sem("prefix_sums_ready")
        s_gelu = sem("gmlp_gelu_ready")
        s_vn = sem("gmlp_v_ready")
        s_og = sem("gmlp_out_ready")
        s_cv = sem("conv_out_ready")
        s_cvsq = sem("conv_squares_ready")
        s_nmax = sem("row_max_ready")
        s_exp = sem("prob_ready")
        s_pv = sem("head_out_in_psum")
        s_oh = sem("head_out_ready")
        s_x = sem("x_mixed")
        s_sc = sem("exp_scores_ready")
        s_idx = sem("routing_ready")
        s_gexp = sem("gate_logits_ready")
        s_stage = sem("index_staged")
        s_land = [sem(f"slot_landed{n}") for n in range(NBUF)]
        s_dot = sem("dot_ready")
        s_ge = sem("expert_gelu_ready")
        s_w = sem("expert_weight_ready")
        s_dg = sem("diag_ready")
        s_used = sem("slots_free")
        s_acc = sem("experts_summed")
        s_xe = sem("x_with_experts")
        s_out = sem("final_ready")
        s_st = sem("stored")

        def wait_full(eng, l, *key):
            n = turn(l, *key)
            eng.wait_ge(full[n % RING], n // RING + 1)
            return banks[n % RING]

        def wait_free(eng, l, *key):
            n = turn(l, *key)
            if n >= RING:
                eng.wait_ge(free[n % RING], n // RING)
            return banks[n % RING]

        def is_full(ins, l, *key):
            ins.then_inc(full[turn(l, *key) % RING], 1)

        def is_free(ins, l, *key):
            ins.then_inc(free[turn(l, *key) % RING], 1)

        last_turn = [("CC", CC - 1), ("CB", CC - 1), ("G", TILES - 1), ("V", TILES - 1), ("Q", AC - 1), ("K", AC - 1)]
        last_turn += [("OC", f, TILES - 1) for f in range(N_OUT)]
        last_turn += [("QY", (f + 1) * (SLAB // P) - 1) for f in range(NQ)]
        rms_of_layer = [rstd, gr, rm, rstd]
        RMS = len(rms_of_layer)

        def acc_banks(t):
            return banks[6:8] if t % 2 == 0 else banks[4:6]

        def slab_no(l, s):
            return l * SLABS + s

        def slab_view(l, s, cols=SLAB):
            return slabs[slab_no(l, s) % NSLAB][:, 0:DC * cols].rearrange("p (c n) -> p c n", c=DC)

        def wait_slab(eng, l, s):
            n = slab_no(l, s)
            loads = sum(2 if m % SLABS == 0 else 1 for m in range(n % NSLAB, n + 1, NSLAB))
            eng.wait_ge(s_slab[n % NSLAB], 16 * loads)

        UNITS_T = TILES * UNITS
        block = ctx.enter_context(nc.Block())

        @block.sync
        def _(sp):
            sp.dma_start(x[:], x_d.rearrange("(i p) d -> p i d", p=P)).then_inc(s_const, 16)
            for l in range(L):
                def parameters():
                    if l:
                        sp.wait_ge(s_xe, l * TILES)
                    sp.dma_start(gain[:], norm1_g[l:l + 1, :].broadcast_to([P, D])).then_inc(s_gain, 16)
                    sp.dma_start(sgu_b[:], sgu_g[l:l + 1, :].broadcast_to([P, GW])).then_inc(s_layer, 16)
                    sp.dma_start(wsp[:], w_spatial[l]).then_inc(s_layer, 16)
                    sp.dma_start(bsp[:], b_spatial[l]).then_inc(s_layer, 16)
                    sp.dma_start(mixg[:], mix_g[l]).then_inc(s_layer, 16)
                    sp.dma_start(cw[:], conv_w[l]).then_inc(s_layer, 16)
                    sp.dma_start(bf[:], b_forget[l].unsqueeze(1)).then_inc(s_layer, 16)
                    sp.dma_start(keysT[:], sub_keys[l]).then_inc(s_layer, 16)

                if l == 0:
                    parameters()
                for s in range(SLABS):
                    if l and s == NSLAB:
                        parameters()
                    n = slab_no(l, s)
                    if n >= NSLAB:
                        m = turn((n - NSLAB) // SLABS, *last_turn[(n - NSLAB) % SLABS])
                        sp.wait_ge(free[m % RING], m // RING + 1)
                    arrived = s_slab[n % NSLAB]
                    if s == S_F:
                        dst = slab_view(l, s, H + CW)
                        sp.dma_start(dst[:, :, 0:H], w_in[l, :, :, O_F:O_F + H]).then_inc(arrived, 16)
                        sp.dma_start(dst[:, :, H:H + CW],
                                     w_in[l, :, :, O_C + 2 * CW:O_C + 3 * CW]).then_inc(arrived, 16)
                    elif s < N_IN:
                        o = {S_C: O_C, S_G: O_G, S_V: O_V, S_Q: O_Q, S_K: O_K}[s]
                        sp.dma_start(slab_view(l, s), w_in[l, :, :, o:o + SLAB]).then_inc(arrived, 16)
                    elif s < S_QY:
                        o = (s - S_O) * SLAB
                        sp.dma_start(slab_view(l, s), w_out[l, :, :, o:o + SLAB]).then_inc(arrived, 16)
                    else:
                        o = (s - S_QY) * SLAB
                        sp.dma_start(slab_view(l, s), w_query[l, :, :, o:o + SLAB]).then_inc(arrived, 16)
                    if s == S_O:
                        sp.wait_ge(s_h, 2 * l * TILES + TILES)
                        sp.dma_start(gain[:], norm2_g[l:l + 1, :].broadcast_to([P, D])).then_inc(s_gain, 16)
            sp.wait_ge(s_acc, (L - 1) * TILES + 1)
            sp.dma_start(gain[:], final_g.rearrange("(a d) -> a d", a=1).broadcast_to([P, D]))\
              .then_inc(s_gain, 16)
            for i in range(TILES):
                sp.wait_ge(s_out, i + 1)
                sp.dma_start(out_d[i * P:(i + 1) * P, :], h_nat[:, i, :]).then_inc(s_st, 16)
            sp.wait_ge(s_st, 16 * TILES)

        @block.gpsimd
        def _(pool):
            nc.gpsimd.memset(ident[:], 0.0).then_inc(s_setup, 1)
            nc.gpsimd.memset(causal[:], 0.0).then_inc(s_setup, 1)
            nc.gpsimd.memset(zero16[:], 0.0).then_inc(s_setup, 1)
            nc.gpsimd.memset(ones[:], 1.0).then_inc(s_setup, 1)
            nc.gpsimd.memset(neghalf[:], -0.5).then_inc(s_setup, 1)
            nc.gpsimd.iota(iota[:], pattern=[[1, K]], base=0, channel_multiplier=0,
                           allow_small_or_imprecise_dtypes=True).then_inc(s_setup, 1)
            pool.wait_ge(s_setup, 6)
            nc.gpsimd.affine_select(out=ident[:], in_=ident[:], compare_op=ALU.not_equal, fill=1.0, base=0,
                                    pattern=[[-1, P]], channel_multiplier=1).then_inc(s_setup, 1)
            nc.gpsimd.affine_select(out=causal[:], in_=causal[:], compare_op=ALU.is_ge, fill=MASKED / SCALE,
                                    base=0, pattern=[[-1, P]], channel_multiplier=1).then_inc(s_setup, 1)
            pool.wait_ge(s_setup, 8)
            nc.gpsimd.tensor_copy(ident16[:], ident[:]).then_inc(s_setup, 1)
            def inverse_roots(n, dst):
                pool.wait_ge(s_ms, n + 1)
                nc.gpsimd.tensor_tensor(dst, dst, neghalf[:, 0:dst.shape[1]], ALU.pow).then_inc(s_rms, 1)

            def gather_chunk(n0, t, c0):
                with pool.Fori(0, CS // BODY) as it:
                    for b in range(BODY):
                        j = b % NBUF
                        pool.wait_ge(s_used, it * BODY + (n0 + b + 1))
                        pool.nop(nofuse=True)
                        nc.gpsimd.tensor_copy(stage[:, j:j + 1],
                                              eidx[:, t % 2, bass.ds(it * BODY + (c0 + b), 1)])\
                          .then_inc(s_stage, 1)
                        pool.wait_ge(s_stage, it * BODY + (n0 + b + 1))
                        pool.nop(nofuse=True)
                        nc.gpsimd.indirect_dma_start(
                            arena[:, j, :], None, uv,
                            bass.IndirectOffsetOnAxis(ap=stage[:, j:j + 1], axis=0)).then_inc(s_land[j], 16)

            for l in range(L):
                pool.wait_ge(s_layer, 16 * 7 * (l + 1))
                nc.gpsimd.affine_select(out=wsp[:], in_=wsp[:], compare_op=ALU.is_ge, fill=0.0, base=0,
                                        pattern=[[0, GG], [1, P]], channel_multiplier=-1).then_inc(s_setup, 1)
                for k, dst in enumerate(rms_of_layer):
                    inverse_roots(l * RMS + k, dst)
                for t in range(TILES):
                    n0 = (l * TILES + t) * SLOTS
                    for c in range(2):
                        pool.wait_ge(s_idx, chunk_no(l, t, c) + 1)
                        gather_chunk(n0 + c * CS, t, c * CS)
            inverse_roots(L * RMS, rstd)

        @block.scalar
        def _(act):
            steps = [0]

            def step(ins):
                steps[0] += 1
                ins.then_inc(s_act, 1)
                act.wait_ge(s_act, steps[0])

            def copy_out(dst, l, *key, scale=1.0):
                b = wait_full(act, l, *key)
                n = 1
                for s in dst.shape[1:]:
                    n *= s
                is_free(nc.scalar.activation(dst, b[0:dst.shape[0], 0:n].rearrange("p (a b) -> p a b", a=dst.shape[1])
                                             if len(dst.shape) == 3 else b[0:dst.shape[0], 0:n],
                                             ACT.Copy, scale=scale), l, *key)

            squared = [0]

            def square(src, total):
                if squared[0]:
                    act.wait_ge(s_sq, squared[0])
                squared[0] += 1
                nc.scalar.activation(junk[:, 0:src.shape[1]], src, ACT.Square, accum_out=total).then_inc(s_sq, 1)

            act.wait_ge(s_const, 16)
            for l in range(L):
                if l:
                    act.wait_ge(s_xe, l * TILES)
                for i in range(TILES):
                    square(x[:, i, :], ss[:, i:i + 1])
                for i in range(TILES):
                    copy_out(wide[:, 0:DC // 2, i * P:(i + 1) * P], l, "T1", i, 0)
                act.wait_ge(s_zf, l + 1)
                step(nc.scalar.activation(zf[0:H, 1, :], zf[0:H, 1, :], ACT.Exp))
                nc.scalar.activation(zf[0:H, 1, :], zf[0:H, 1, :], ACT.Ln, bias=1.0).then_inc(s_sp, 1)
                for c in range(CC):
                    copy_out(c_c[:, c, :], l, "CC", c)
                for i in range(TILES):
                    b = wait_full(act, l, "G", i)
                    nc.scalar.activation(ug[:, i, :], b[:], ACT.Gelu_apprx_tanh)\
                      .then_inc(free[turn(l, "G", i) % RING], 1)
                for c in range(CC):
                    act.wait_ge(s_cv, l * CC + c + 1)
                    nc.scalar.activation(c_c[:, c, :], y_cv[:, c, :], ACT.Square).then_inc(s_cvsq, 1)
                for i in range(TILES):
                    copy_out(v_nat[:, i, :], l, "V", i)
                for c in range(AC):
                    copy_out(kT[:, c, :], l, "K", c)
                for h in range(0, H, 2):
                    copy_out(negF[:, h, :], l, "FB", h, scale=-1.0 / SCALE)
                for i in range(TILES):
                    act.wait_ge(s_og, l * TILES + i + 1)
                    square(ug[:, i, 0:GW], ssm[:, 4 + i:5 + i])
                for s in range(UN + O_LAG):
                    if s < UN:
                        d, W = s % DEEP, (s // H + 1) * P
                        act.wait_ge(s_nmax, l * UN + s + 1)
                        nc.scalar.activation(prob[:, d, 0:W], logit[:, d, 0:W], ACT.Exp, bias=nmax[:, d:d + 1],
                                             accum_out=rsum[:, d:d + 1]).then_inc(s_exp, 1)
                    if T_LAG <= s < UN + T_LAG:
                        v = s - T_LAG
                        copy_out(probT[:, v % 2, 0:(v // H + 1) * P], l, "P", v)
                    if s >= O_LAG and (s - O_LAG) % H == H - 1:
                        act.wait_ge(s_oh, l * UN + s - O_LAG + 1)
                        i = (s - O_LAG) // H
                        square(o_att[:, i % 2, :], ssm[:, i:i + 1])
                for i in range(TILES):
                    act.wait_ge(s_x, l * TILES + i + 1)
                    square(x[:, i, :], ss[:, i:i + 1])
                for i in range(TILES):
                    copy_out(wide[:, 0:DC // 2, i * P:(i + 1) * P], l, "T2", i, 0)
                def gate_exp(t, c):
                    act.wait_ge(s_gexp, chunk_no(l, t, c) + 1)
                    top = scratch(t, c).top
                    nc.scalar.activation(top, top, ACT.Exp).then_inc(s_sc, 1)

                for c in range(UNITS):
                    copy_out(qyT[:, c % 2, :], l, "QY", c)
                    if c == 2 * HC + 4:
                        gate_exp(0, 0)
                for t in range(TILES):
                    for q in range(PARTS):
                        if q == PARTS // 2 - 1:
                            gate_exp(t, 1)
                        if q == PARTS - 1 and t + 1 < TILES:
                            gate_exp(t + 1, 0)
                        if q % (PARTS // 2) == 0:
                            act.wait_ge(s_idx, chunk_no(l, t, q // (PARTS // 2)) + 1)
                        c0 = q * LOOP * BODY
                        n0 = (l * TILES + t) * SLOTS + c0
                        with act.Fori(0, LOOP) as it:
                            nc.scalar.activation(gstage[:], gate[:, t % 2, bass.ds(it * BODY + c0, BODY)], ACT.Copy)
                            for b in range(0, BODY, GROUP):
                                group = slice(b, b + GROUP)
                                done = n0 + b + GROUP
                                act.wait_ge(s_dot, it * BODY + done)
                                nc.scalar.activation(gelu[:, group], dots[:, group], ACT.Gelu_apprx_tanh)\
                                  .then_inc(s_ge, GROUP)
                                act.wait_ge(s_ge, it * BODY + done)
                                for k in range(b, b + GROUP):
                                    nc.scalar.activation(wts[:, k:k + 1], gelu[:, k:k + 1], ACT.Copy,
                                                         scale=gstage[:, k:k + 1]).then_inc(s_w, 1)
                                act.wait_ge(s_w, it * BODY + done)
                                for k in range(b, b + GROUP):
                                    act.wait_ge(s_used, it * BODY + (n0 + k + 1))
                                    nc.scalar.activation(diag[:, k % NBUF, :], ident[:], ACT.Copy,
                                                         scale=wts[:, k:k + 1]).then_inc(s_dg, 1)
            for i in range(TILES):
                act.wait_ge(s_xe, (L - 1) * TILES + i + 1)
                square(x[:, i, :], ss[:, i:i + 1])

        @block.vector
        def _(dve):
            V = nc.vector
            steps = [0]
            squares = [0]

            def step(ins):
                steps[0] += 1
                ins.then_inc(s_vec, 1)
                dve.wait_ge(s_vec, steps[0])

            def copy_out(dst, l, *key):
                b = wait_full(dve, l, *key)
                n = 1
                for s in dst.shape[1:]:
                    n *= s
                src = b[:, 0:n].rearrange("p (a b) -> p a b", a=dst.shape[1]) if len(dst.shape) == 3 else b[:, 0:n]
                is_free(V.tensor_copy(dst, src), l, *key)

            roots = [0]

            def mean_square(dst, src, width):
                return V.tensor_scalar(dst, src, 1.0 / width, EPS, ALU.mult, ALU.add)

            def wait_roots(ins):
                ins.then_inc(s_ms, 1)
                roots[0] += 1
                dve.wait_ge(s_rms, roots[0])

            def norm_scales():
                squares[0] += TILES
                dve.wait_ge(s_sq, squares[0])
                wait_roots(mean_square(rstd, ss, D))

            def norm(i):
                return V.scalar_tensor_tensor(out=h_nat[:, i, :], in0=x[:, i, :], scalar=rstd[:, i:i + 1],
                                              in1=gain[:], op0=ALU.mult, op1=ALU.mult)

            def topk_head(t, h):
                w, k = scratch(t, h // HC), h % HC
                for half in range(2):
                    s, v, n = scores[:, t, 2 * h + half, :], w.vals[:, 2 * k + half, :], w.kidx[:, 2 * k + half, :]
                    step(V.max(v[:, 0:8], s))
                    V.max_index(n[:, 0:8], v[:, 0:8], s)
                    step(V.match_replace(s, v[:, 0:8], s, NEG))
                    step(V.max(v[:, 8:16], s))
                    step(V.max_index(n[:, 8:16], v[:, 8:16], s))
                s, v, n = w.cand, w.top[:, k, :], w.tidx[:, k, :]
                step(V.tensor_tensor(s.rearrange("p (a b) -> p a b", a=K),
                                     w.vals[:, 2 * k, :].unsqueeze(2).broadcast_to([P, K, K]),
                                     w.vals[:, 2 * k + 1, :].unsqueeze(1).broadcast_to([P, K, K]), ALU.add))
                step(V.max(v[:, 0:8], s))
                V.max_index(n[:, 0:8], v[:, 0:8], s)
                step(V.match_replace(s, v[:, 0:8], s, NEG))
                step(V.max(v[:, 8:16], s))
                step(V.max_index(n[:, 8:16], v[:, 8:16], s))

            def expert_numbers(l, t, c):
                w = scratch(t, c)
                step(V.tensor_copy(dn[:, 0:HC], w.top[:, :, 0]))
                V.tensor_tensor(w.top, w.top, dn[:, 0:HC].unsqueeze(2).broadcast_to([P, HC, K]),
                                ALU.subtract).then_inc(s_gexp, 1)
                places = w.tidx.rearrange("p h k -> p (h k)")
                oh = w.onehot.rearrange("p (a b) -> p a b", b=K)
                oh4 = w.onehot.rearrange("p (h a b) -> p h a b", h=HC, b=K)
                for half in range(2):
                    if half == 0:
                        step(V.tensor_scalar(w.tsel, places, 4, None, ALU.logical_shift_right))
                    else:
                        step(V.tensor_scalar(w.tsel, places, 15, None, ALU.bitwise_and))
                    V.tensor_copy(w.tself, w.tsel)
                    ep = w.epart[:, half, :]
                    ep3 = ep.rearrange("p (h k) -> p h k", h=HC)
                    step(V.tensor_copy(ep3, w.kidx.rearrange("p (h f) k -> p h f k", f=2)[:, :, half, :]))
                    step(V.tensor_tensor(oh, iota[:].unsqueeze(1).broadcast_to([P, CS, K]),
                                         w.tself.unsqueeze(2).broadcast_to([P, CS, K]), ALU.is_equal))
                    step(V.tensor_tensor(oh4, oh4, ep3.unsqueeze(2).broadcast_to([P, HC, K, K]), ALU.mult))
                    step(V.tensor_reduce(ep, oh, AX.X, ALU.add))
                step(V.scalar_tensor_tensor(out=w.epart[:, 0, :], in0=w.epart[:, 0, :], scalar=float(KEYS),
                                            in1=w.epart[:, 1, :], op0=ALU.mult, op1=ALU.add))
                step(V.tensor_scalar(w.epart[:, 0, :], w.epart[:, 0, :], float(l * NE), None, ALU.add))
                step(V.tensor_copy(eidx[:, t % 2, c * CS:(c + 1) * CS], w.epart[:, 0, :]))

            def gates(l, t, c):
                w = scratch(t, c)
                dve.wait_ge(s_sc, chunk_no(l, t, c) + 1)
                step(V.tensor_reduce(dn[:, 0:HC], w.top, AX.X, ALU.add))
                step(V.reciprocal(dn[:, 0:HC], dn[:, 0:HC]))
                V.tensor_tensor(gate[:, t % 2, c * CS:(c + 1) * CS].rearrange("p (h k) -> p h k", h=HC), w.top,
                                dn[:, 0:HC].unsqueeze(2).broadcast_to([P, HC, K]), ALU.mult).then_inc(s_idx, 1)

            def routing_part(l, t, q):
                t, c = (t, 1) if q < PARTS // 2 else (t + 1, 0)
                if t < TILES:
                    for k in ((0,), (1,), (2, 3), ())[q % 4]:
                        topk_head(t, c * HC + k)
                    if q % 4 == 3:
                        expert_numbers(l, t, c)
                        gates(l, t, c)

            def add_experts(l, t):
                dve.wait_ge(s_acc, l * TILES + t + 1)
                for f in range(2):
                    xs = x[:, t, f * 512:(f + 1) * 512]
                    ins = V.tensor_tensor(xs, acc_banks(t)[f][:], xs, ALU.add)
                ins.then_inc(s_xe, 1)

            dve.wait_ge(s_const, 16)
            for l in range(L):
                dve.wait_ge(s_gain, 16 * (2 * l + 1))
                dve.wait_ge(s_layer, 16 * 7 * (l + 1))
                norm_scales()
                for i in range(TILES):
                    norm(i).then_inc(s_h, 1)
                    if i:
                        copy_out(wide[:, DC // 2:DC, (i - 1) * P:i * P], l, "T1", i - 1, 1)
                copy_out(wide[:, DC // 2:DC, (TILES - 1) * P:TILES * P], l, "T1", TILES - 1, 1)
                b = wait_full(dve, l, "ZF")
                for c in range(CC):
                    V.memset(zpad[:, c, 0:2], 0.0)
                is_free(V.tensor_scalar(zf[0:H, 0, :], b[0:H, :], bf[:, 0:1], None, ALU.add), l, "ZF")
                dve.wait_ge(free[turn(l, "ZF") % RING], turn(l, "ZF") // RING + 1)
                V.scalar_tensor_tensor(out=zf[0:H, 1, :], in0=zf[0:H, 0, :], scalar=-1.0, in1=zf[0:H, 0, :],
                                       op0=ALU.mult, op1=ALU.min).then_inc(s_zf, 1)
                for c in range(CC):
                    b = wait_full(dve, l, "CI", c)
                    if c == 0:
                        for k in range(CC):
                            n = turn(l, "CC", k)
                            dve.wait_ge(free[n % RING], n // RING + 1)
                    is_free(V.tensor_tensor(zpad[:, c, 2:T + 2], b[:], c_c[:, c, :], ALU.mult), l, "CI", c)
                for c in range(CC):
                    n = turn(l, "CI", c)
                    dve.wait_ge(free[n % RING], n // RING + 1)
                    y = y_cv[:, c, :]
                    step(V.tensor_scalar(y, zpad[:, c, 0:T], cw[:, 0, c:c + 1], None, ALU.mult))
                    step(V.scalar_tensor_tensor(out=y, in0=zpad[:, c, 1:T + 1], scalar=cw[:, 1, c:c + 1], in1=y,
                                                op0=ALU.mult, op1=ALU.add))
                    step(V.scalar_tensor_tensor(out=y, in0=zpad[:, c, 2:T + 2], scalar=cw[:, 2, c:c + 1], in1=y,
                                                op0=ALU.mult, op1=ALU.add))
                    b = wait_full(dve, l, "CB", c)
                    is_free(V.tensor_tensor(y, b[:], y, ALU.mult), l, "CB", c)
                    n = turn(l, "CB", c)
                    dve.wait_ge(free[n % RING], n // RING + 1)
                    V.tensor_scalar(mixT[:, AC + GC + c, :], y, mixg[:, AC + GC + c:AC + GC + c + 1], None,
                                    ALU.mult).then_inc(s_cv, 1)
                dve.wait_ge(s_sp, l + 1)
                step(V.scalar_tensor_tensor(out=zf[0:H, 2, :], in0=zf[0:H, 0, :], scalar=0.0, in1=zf[0:H, 1, :],
                                            op0=ALU.min, op1=ALU.subtract))
                step(V.memset(zf[0:H, 0, :], 1.0))
                V.tensor_tensor_scan(zf[0:H, 3, :], zf[0:H, 0, :], zf[0:H, 2, :], 0.0, ALU.mult, ALU.add)\
                 .then_inc(s_F, 1)
                for i in range(TILES):
                    n = turn(l, "G", i)
                    dve.wait_ge(free[n % RING], n // RING + 1)
                    gv = ug[:, i, GW:2 * GW]
                    step(V.tensor_tensor(vn[:, i, :], gv, gv, ALU.mult))
                    step(V.tensor_reduce(gs[:, i * GG:(i + 1) * GG], vn[:, i, :].rearrange("p (g d) -> p g d", g=GG),
                                         AX.X, ALU.add))
                wait_roots(mean_square(gr, gs, GD))
                for i in range(TILES):
                    vi = vn[:, i, :]
                    step(V.tensor_tensor(vi.rearrange("p (g d) -> p g d", g=GG),
                                         ug[:, i, GW:2 * GW].rearrange("p (g d) -> p g d", g=GG),
                                         gr[:, i * GG:(i + 1) * GG].unsqueeze(2).broadcast_to([P, GG, GD]), ALU.mult))
                    V.tensor_tensor(vi, vi, sgu_b[:], ALU.mult).then_inc(s_vn, 1)
                for c in range(AC):
                    copy_out(qT[:, c, :], l, "Q", c)
                for h in range(1, H, 2):
                    b = wait_full(dve, l, "FB", h)
                    is_free(V.tensor_scalar(negF[:, h, :], b[:], -1.0 / SCALE, None, ALU.mult), l, "FB", h)
                for i in range(TILES):
                    b = wait_full(dve, l, "GM", i)
                    for g in range(GG):
                        sl = slice(g * GD, (g + 1) * GD)
                        ins = V.scalar_tensor_tensor(out=ug[:, i, sl], in0=b[:, sl], scalar=bsp[:, g:g + 1],
                                                     in1=ug[:, i, sl], op0=ALU.add, op1=ALU.mult)
                    is_free(ins, l, "GM", i)
                    n = turn(l, "GM", i)
                    dve.wait_ge(free[n % RING], n // RING + 1)
                    dve.nop().then_inc(s_og, 1)
                b = wait_full(dve, l, "CS")
                is_free(V.tensor_copy(ssm[:, 8:8 + TILES], b[:, 0:TILES]), l, "CS")
                for i in range(TILES):
                    b = wait_full(dve, l, "GT", i)
                    is_free(V.tensor_tensor(mixT[:, AC:AC + GC, i * P:(i + 1) * P],
                                            b[:, 0:GC * P].rearrange("p (c n) -> p c n", c=GC),
                                            mixg[:, AC:AC + GC].unsqueeze(2).broadcast_to([P, GC, P]), ALU.mult),
                            l, "GT", i)
                for h in range(0, H, 2):
                    n = turn(l, "FB", h)
                    dve.wait_ge(free[n % RING], n // RING + 1)
                for s in range(UN + AT_LAG):
                    if s < UN:
                        h, d, W = s % H, s % DEEP, (s // H + 1) * P
                        b = wait_full(dve, l, "S", s)
                        if s >= DEEP:
                            dve.wait_ge(s_exp, l * UN + s - DEEP + 1)
                        is_free(V.tensor_tensor_reduce(out=logit[:, d, 0:W], in0=b[:, 0:W], in1=negF[:, h, 0:W],
                                                       scale=SCALE, scalar=-3.0e38, op0=ALU.add, op1=ALU.max,
                                                       accum_out=rmax[:, d:d + 1]), l, "S", s)
                        n = turn(l, "S", s)
                        dve.wait_ge(free[n % RING], n // RING + 1)
                        V.tensor_scalar(nmax[:, d:d + 1], rmax[:, d:d + 1], -1.0, None, ALU.mult).then_inc(s_nmax, 1)
                    if O_LAG <= s < UN + O_LAG:
                        w = s - O_LAG
                        i, h = w // H, w % H
                        dve.wait_ge(s_pv, l * UN + w + 1)
                        if w >= 2 * H and h == 0:
                            dve.wait_ge(s_sq, squares[0] + TILES + (i - 2) + 1)
                        V.tensor_scalar(o_att[:, i % 2, h * DH:(h + 1) * DH], banks[6 + w % 2][:, 0:DH],
                                        rinv[:, w % DEEP:w % DEEP + 1], None, ALU.mult).then_inc(s_oh, 1)
                    if T_LAG <= s < UN + T_LAG:
                        w = s - T_LAG
                        dve.wait_ge(s_exp, l * UN + w + 1)
                        step(V.reciprocal(rinv[:, w % DEEP:w % DEEP + 1], rsum[:, w % DEEP:w % DEEP + 1]))
                    if s >= AT_LAG and (s - AT_LAG) % H == H - 1:
                        i = (s - AT_LAG) // H
                        b = wait_full(dve, l, "AT", i)
                        is_free(V.tensor_tensor(mixT[:, 0:AC, i * P:(i + 1) * P],
                                                b[:].rearrange("p (c n) -> p c n", c=AC),
                                                mixg[:, 0:AC].unsqueeze(2).broadcast_to([P, AC, P]), ALU.mult),
                                l, "AT", i)
                squares[0] += 2 * TILES
                dve.wait_ge(s_sq, squares[0])
                n = turn(l, "CS")
                dve.wait_ge(free[n % RING], n // RING + 1)
                step(mean_square(rm[:, 0:4], ssm[:, 0:4], AW))
                step(mean_square(rm[:, 4:8], ssm[:, 4:8], GW))
                wait_roots(mean_square(rm[:, 8:12], ssm[:, 8:12], CW))
                for f in range(N_OUT):
                    for i in range(TILES):
                        xs = x[:, i, f * SLAB:(f + 1) * SLAB]
                        for k, key in enumerate(("OA", "OG", "OC")):
                            b = wait_full(dve, l, key, f, i)
                            ins = V.scalar_tensor_tensor(out=xs, in0=b[:], scalar=rm[:, 4 * k + i:4 * k + i + 1], in1=xs,
                                                         op0=ALU.mult, op1=ALU.add)
                            is_free(ins, l, key, f, i)
                            n = turn(l, key, f, i)
                            dve.wait_ge(free[n % RING], n // RING + 1)
                        if f == N_OUT - 1:
                            dve.nop().then_inc(s_x, 1)
                dve.wait_ge(s_gain, 16 * (2 * l + 2))
                norm_scales()
                for i in range(TILES):
                    norm(i).then_inc(s_h, 1)
                    if i:
                        copy_out(wide[:, DC // 2:DC, (i - 1) * P:i * P], l, "T2", i - 1, 1)
                copy_out(wide[:, DC // 2:DC, (TILES - 1) * P:TILES * P], l, "T2", TILES - 1, 1)
                for c in range(UNITS):
                    copy_out(scores[:, :, c, :], l, "SC", c)
                    if c % 2 and 3 <= c < 2 * HC + 3:
                        h = (c - 3) // 2
                        for k in (2 * h, 2 * h + 1):
                            n = turn(l, "SC", k)
                            dve.wait_ge(free[n % RING], n // RING + 1)
                        topk_head(0, h)
                    if c == 2 * HC + 3:
                        expert_numbers(l, 0, 0)
                    if c == 2 * HC + 5:
                        gates(l, 0, 0)
                for c in range(UNITS - 4, UNITS):
                    n = turn(l, "SC", c)
                    dve.wait_ge(free[n % RING], n // RING + 1)
                for t in range(TILES):
                    for q in range(PARTS):
                        n0 = (l * TILES + t) * SLOTS + q * LOOP * BODY
                        routing_part(l, t, q)
                        with dve.Fori(0, LOOP) as it:
                            for b in range(BODY):
                                dve.wait_ge(s_land[b % NBUF], it * (16 * BODY // NBUF) + 16 * ((n0 + b) // NBUF + 1))
                                uu = arena[:, b % NBUF, 0:D]
                                V.tensor_tensor_reduce(out=uu, in0=uu, in1=h_nat[:, t, :], scale=1.0, scalar=0.0,
                                                       op0=ALU.mult, op1=ALU.add,
                                                       accum_out=dots[:, b:b + 1])\
                                 .then_inc(s_dot, 1)
                        if q == 0 and t:
                            add_experts(l, t - 1)
                add_experts(l, TILES - 1)
                dve.wait_ge(s_xe, (l + 1) * TILES)
            dve.wait_ge(s_gain, 16 * (2 * L + 1))
            norm_scales()
            for i in range(TILES):
                norm(i).then_inc(s_out, 1)

        @block.tensor
        def _(pe):
            def mm(out, lhsT, rhs, start, stop):
                return nc.tensor.matmul(out, lhsT, rhs, start=start, stop=stop)

            def transposes(l, i, name, f):
                b = wait_free(pe, l, name, i, f)
                for c in range(DC // 2):
                    col = (f * (DC // 2) + c) * P
                    ins = nc.tensor.transpose(b[:, c * P:(c + 1) * P], h_nat[:, i, col:col + P], ident[:])
                is_full(ins, l, name, i, f)

            def feature_major(l, s, cols, c0, m, *key):
                b = wait_free(pe, l, *key)
                w = slab_view(l, s, cols)
                for c in range(DC):
                    ins = mm(b[0:m, :], w[:, c, c0:c0 + m], wide[:, c, :], c == 0, c == DC - 1)
                is_full(ins, l, *key)

            def token_major(l, s, i, *key):
                b = wait_free(pe, l, *key)
                w = slab_view(l, s)
                for c in range(DC):
                    ins = mm(b[:], wide[:, c, i * P:(i + 1) * P], w[:, c, :], c == 0, c == DC - 1)
                is_full(ins, l, *key)

            def zeros(bank, opens):
                for c in range(4):
                    ins = mm(bank[:, c * P:(c + 1) * P], ident16[:], zero16[:], opens and c == 0,
                             not opens and c == 3)
                return ins

            def in_sbuf(l, *key):
                n = turn(l, *key)
                pe.wait_ge(free[n % RING], n // RING + 1)

            pe.wait_ge(s_setup, 9)
            pe.nop().then_inc(s_used, NBUF)
            for l in range(L):
                if l:
                    pe.wait_ge(s_xe, l * TILES)
                for i in range(TILES):
                    pe.wait_ge(s_h, 2 * l * TILES + i + 1)
                    for f in range(2):
                        transposes(l, i, "T1", f)
                for i in range(TILES):
                    for f in range(2):
                        in_sbuf(l, "T1", i, f)
                wait_slab(pe, l, S_F)
                feature_major(l, S_F, H + CW, 0, H, "ZF")
                for c in range(CC):
                    feature_major(l, S_F, H + CW, H + c * P, P, "CC", c)
                wait_slab(pe, l, S_C)
                for c in range(CC):
                    feature_major(l, S_C, SLAB, c * P, P, "CI", c)
                for c in range(CC):
                    feature_major(l, S_C, SLAB, CW + c * P, P, "CB", c)
                for name, s in (("G", S_G), ("V", S_V)):
                    wait_slab(pe, l, s)
                    for i in range(TILES):
                        token_major(l, s, i, name, i)
                for name, s in (("Q", S_Q), ("K", S_K)):
                    wait_slab(pe, l, s)
                    for c in range(AC):
                        feature_major(l, s, SLAB, c * P, P, name, c)
                pe.wait_ge(s_F, l + 1)
                for h in range(H):
                    b = wait_free(pe, l, "FB", h)
                    is_full(mm(b[:], ident[0:H, h:h + 1].broadcast_to([H, P]), zf[0:H, 3, :], True, True), l, "FB", h)
                pe.wait_ge(s_setup, 10 + l)
                for i in range(TILES):
                    pe.wait_ge(s_vn, l * TILES + i + 1)
                    b = wait_free(pe, l, "GM", i)
                    for g in range(GG):
                        ins = mm(b[:, g * GD:(g + 1) * GD], wsp[:, g, :], vn[:, i, g * GD:(g + 1) * GD], True, True)
                    is_full(ins, l, "GM", i)
                pe.wait_ge(s_cvsq, (l + 1) * CC)
                b = wait_free(pe, l, "CS")
                for i in range(TILES):
                    for c in range(CC):
                        ins = mm(b[:, i:i + 1], c_c[:, c, i * P:(i + 1) * P], ones[:, 0:1], c == 0, c == CC - 1)
                is_full(ins, l, "CS")
                for i in range(TILES):
                    pe.wait_ge(s_og, l * TILES + i + 1)
                    b = wait_free(pe, l, "GT", i)
                    for c in range(GC):
                        ins = nc.tensor.transpose(b[:, c * P:(c + 1) * P], ug[:, i, c * P:(c + 1) * P], ident[:])
                    is_full(ins, l, "GT", i)
                for i in range(TILES):
                    in_sbuf(l, "V", i)
                for c in range(AC):
                    in_sbuf(l, "Q", c)
                    in_sbuf(l, "K", c)
                for s in range(UN + AT_LAG):
                    if s < UN:
                        i, h = s // H, s % H
                        W = (i + 1) * P
                        r = slice((h % 2) * DH, (h % 2) * DH + DH)
                        b = wait_free(pe, l, "S", s)
                        mm(b[:, 0:W], qT[r, h // 2, i * P:(i + 1) * P], kT[r, h // 2, 0:W], True, False)
                        is_full(mm(b[:, W - P:W], ident16[:], causal[:], False, True), l, "S", s)
                    if T_LAG <= s < UN + T_LAG:
                        v = s - T_LAG
                        pe.wait_ge(s_exp, l * UN + v + 1)
                        b = wait_free(pe, l, "P", v)
                        for c in range(v // H + 1):
                            ins = nc.tensor.transpose(b[:, c * P:(c + 1) * P], prob[:, v % DEEP, c * P:(c + 1) * P],
                                                      ident[:])
                        is_full(ins, l, "P", v)
                    if V_LAG <= s < UN + V_LAG:
                        w = s - V_LAG
                        i, h = w // H, w % H
                        in_sbuf(l, "P", w)
                        if w >= 2:
                            pe.wait_ge(s_oh, l * UN + w - 1)
                        for c in range(i + 1):
                            ins = mm(banks[6 + w % 2][:, 0:DH], probT[:, w % 2, c * P:(c + 1) * P],
                                     v_nat[:, c, h * DH:(h + 1) * DH], c == 0, c == i)
                        ins.then_inc(s_pv, 1)
                    if s >= AT_LAG and (s - AT_LAG) % H == H - 1:
                        i = (s - AT_LAG) // H
                        pe.wait_ge(s_oh, l * UN + (i + 1) * H)
                        b = wait_free(pe, l, "AT", i)
                        for c in range(AC):
                            ins = nc.tensor.transpose(b[:, c * P:(c + 1) * P], o_att[:, i % 2, c * P:(c + 1) * P],
                                                      ident[:])
                        is_full(ins, l, "AT", i)
                for i in range(TILES):
                    in_sbuf(l, "AT", i)
                    in_sbuf(l, "GT", i)
                for f in range(N_OUT):
                    wait_slab(pe, l, S_O + f)
                    w = slab_view(l, S_O + f)
                    for i in range(TILES):
                        for key, lo, hi in (("OA", 0, AC), ("OG", AC, AC + GC), ("OC", AC + GC, DC)):
                            b = wait_free(pe, l, key, f, i)
                            for c in range(lo, hi):
                                ins = mm(b[:], mixT[:, c, i * P:(i + 1) * P], w[:, c, :], c == lo, c == hi - 1)
                            is_full(ins, l, key, f, i)
                for i in range(TILES):
                    pe.wait_ge(s_h, (2 * l + 1) * TILES + i + 1)
                    for f in range(2):
                        transposes(l, i, "T2", f)
                for i in range(TILES):
                    for f in range(2):
                        in_sbuf(l, "T2", i, f)

                def unit_scores(c):
                    in_sbuf(l, "QY", c)
                    b = wait_free(pe, l, "SC", c)
                    for i in range(TILES):
                        ins = mm(b[:, i * KEYS:(i + 1) * KEYS], qyT[:, c % 2, i * P:(i + 1) * P], keysT[:, c % 2, :],
                                 True, True)
                    is_full(ins, l, "SC", c)

                per = SLAB // P
                for c in range(UNITS):
                    if c % per == 0:
                        wait_slab(pe, l, S_QY + c // per)
                    feature_major(l, S_QY + c // per, SLAB, (c % per) * P, P, "QY", c)
                    if c:
                        unit_scores(c - 1)
                unit_scores(UNITS - 1)
                for c in range(UNITS - RING // 2 - 1, UNITS):
                    in_sbuf(l, "SC", c)
                for t in range(TILES):
                    if t >= 2:
                        pe.wait_ge(s_xe, l * TILES + t - 1)
                    acc = acc_banks(t)
                    for f in range(2):
                        zeros(acc[f], True)
                    for q in range(PARTS):
                        n0 = (l * TILES + t) * SLOTS + q * LOOP * BODY
                        with pe.Fori(0, LOOP) as it:
                            for b in range(BODY):
                                j = b % NBUF
                                pe.wait_ge(s_dg, it * BODY + (n0 + b + 1))
                                for f in range(2):
                                    ins = nc.tensor.matmul(acc[f][:], diag[:, j, :],
                                                           arena[:, j, D + f * 512:D + (f + 1) * 512],
                                                           start=False, stop=False)
                                ins.then_inc(s_used, 1)
                    for f in range(2):
                        ins = zeros(acc[f], False)
                    ins.then_inc(s_acc, 1)


def kernel(x, norm1_g, w_in, b_forget, sgu_norm_g, w_spatial, b_spatial, conv_w, mix_norm_g, w_out,
           norm2_g, w_query, sub_keys, expert_u, expert_v, final_g):
    import numpy as np
    import concourse.bacc as bacc
    from concourse.bass_utils import run_bass_kernel_spmd as run

    def chunked(w):
        l, d, n = w.shape
        return w.reshape(l, d // P, P, n).transpose(0, 2, 1, 3)

    L, D = norm1_g.shape
    arrays = {
        "x": x.reshape(-1, D),
        "norm1_g": norm1_g,
        "w_in": chunked(w_in),
        "b_forget": b_forget,
        "sgu_g": sgu_norm_g,
        "w_spatial": w_spatial.transpose(0, 3, 1, 2),
        "b_spatial": b_spatial.transpose(0, 2, 1),
        "conv_w": conv_w.reshape(L, conv_w.shape[1], -1, P).transpose(0, 3, 1, 2),
        "mix_g": mix_norm_g.reshape(L, -1, P).transpose(0, 2, 1),
        "w_out": chunked(w_out),
        "norm2_g": norm2_g,
        "w_query": chunked(w_query),
        "sub_keys": sub_keys.transpose(0, 3, 1, 2),
        "uv": np.concatenate([expert_u, expert_v], axis=2).reshape(-1, 2 * D),
        "final_g": final_g,
    }
    nc = bacc.Bacc("TRN2", target_bir_lowering=False, num_devices=1)
    fed, args = {}, []
    for name, a in arrays.items():
        a = np.ascontiguousarray(a)
        fed[f"in_{name}"] = a
        args.append(nc.dram_tensor(f"in_{name}", a.shape, mybir.dt.from_np(a.dtype), kind="ExternalInput").ap())
    out = nc.dram_tensor("out_0", arrays["x"].shape, F32, kind="ExternalOutput").ap()
    trunk_kernel(nc, *args, out)
    r = run(nc, [fed], core_ids=[0])
    return r.results[0]["out_0"].reshape(x.shape)
```

```python
from contextlib import ExitStack

import concourse.bass as bass
from concourse import mybir

ALU = mybir.AluOpType
ACT = mybir.ActivationFunctionType
AX = mybir.AxisListType
F32 = mybir.dt.float32
F32R = mybir.dt.float32r
BF16 = mybir.dt.bfloat16
U32 = mybir.dt.uint32

P = 128
EPS = 1e-6
NEG = -3.0e38
MASKED = -1e30
SLAB = 512
PIECE = 256
NSLAB = 3
RING = 6
T_LAG, V_LAG, O_LAG, AT_LAG = 2, 3, 4, 5
DEEP = 3
NBUF = 8
GROUP = 2
BODY = 8
PARTS = 8
EARLY = 4


def trunk_kernel(nc, x_d, norm1_g, w_in, b_forget, sgu_g, w_spatial, b_spatial, conv_w, mix_g, w_out,
                 norm2_g, w_query, sub_keys, uv, final_g, out_d):
    L = norm1_g.shape[0]
    T, D = x_d.shape
    TILES = T // P
    DC = D // P
    H = b_forget.shape[1]
    AW = D // 2
    DH = AW // H
    GW = sgu_g.shape[1]
    GG = w_spatial.shape[2]
    GD = GW // GG
    CW = conv_w.shape[3] * P
    CC = CW // P
    AC = AW // P
    GC = GW // P
    KEYS = sub_keys.shape[3]
    NE = uv.shape[0] // L
    PH = w_query.shape[3] // 2 // P
    UNITS = 2 * PH
    K = 16
    SLOTS = PH * K
    HC = 2
    CHUNKS = PH // HC
    PC = PARTS // CHUNKS
    CS = HC * K
    SCALE = float(DH) ** -0.5
    NQ = UNITS // (SLAB // P)
    LOOP = SLOTS // PARTS // BODY
    O_Q, O_K, O_V = 0, AW, 2 * AW
    O_F = 3 * AW
    O_G = O_F + H
    O_C = O_G + 2 * GW
    N_IN = 6
    N_OUT = D // SLAB
    SLABS = N_IN + N_OUT + NQ + 1
    S_F, S_C, S_G, S_V, S_Q, S_K, S_O = 0, 1, 2, 3, 4, 5, 6
    S_QY = S_O + N_OUT
    pieces = [(S_F, 0, P, ("ZF",)), (S_F, H, PIECE, ("CC", CC - 1)),
              (S_C, 0, PIECE, ("CI", CC - 1)), (S_C, PIECE, PIECE, ("CB", CC - 1))]
    pieces += [(s, f * PIECE, PIECE, (n, f, TILES - 1)) for n, s in (("G", S_G), ("V", S_V)) for f in range(2)]
    pieces += [(s, f * PIECE, PIECE, (n, (f + 1) * PIECE // P - 1)) for n, s in (("Q", S_Q), ("K", S_K))
               for f in range(2)]
    NP = len(pieces)

    UN = TILES * H
    order = [("T1", i, f) for i in range(TILES) for f in range(2)]
    order += [("ZF",)] + [(n, c) for n in ("CC", "CI", "CB") for c in range(CC)]
    order += [(n, f, i) for n in ("G", "V") for f in range(2) for i in range(TILES)]
    order += [("Q", c) for c in range(AC)] + [("K", c) for c in range(AC)]
    order += [("FB", h) for h in range(H)] + [("GM", i) for i in range(TILES)] + [("CS",)]
    order += [("GT", i) for i in range(TILES)]
    for s in range(UN + AT_LAG):
        order += [("S", s)] if s < UN else []
        order += [("P", s - T_LAG)] if T_LAG <= s < UN + T_LAG else []
        order += [("AT", (s - AT_LAG) // H)] if s >= AT_LAG and (s - AT_LAG) % H == H - 1 else []
    order += [(n, f, i) for f in range(N_OUT) for i in range(TILES) for n in ("OA", "OG", "OC")]
    order += [("T2", i, f) for i in range(2) for f in range(2)] + [("QA", 0)]
    order += [("T2", i, f) for i in range(2, TILES) for f in range(2)] + [("SA", 0), ("QA", 1)]
    for c in range(2, NQ):
        order += [("QA", c), ("SA", c - 1)]
    order += [("QB", 0), ("SA", NQ - 1)]
    for c in range(1, EARLY):
        order += [("QB", c), ("SB", c - 1)]
    order += [("SB", EARLY - 1)]
    def late(q):
        first = EARLY + 2 * (q - 1)
        return range(first, min(first + 2, UNITS)) if q >= 1 else ()

    for q in range(PARTS):
        order += [("QB", c) for c in late(q)] + [("SB", c) for c in late(q - 1)]
    assert not late(PARTS - 1)
    place = {key: n for n, key in enumerate(order)}
    PER = len(order)

    def turn(l, *key):
        return l * PER + place[key]

    ctx = ExitStack()
    with ctx:
        def sb(name, shape, dt=F32):
            return ctx.enter_context(nc.sbuf_tensor(name, shape, dt))

        def sem(name):
            return ctx.enter_context(nc.semaphore(name))

        banks = [ctx.enter_context(nc.psum_tensor(f"bank{n}", [P, 512], F32)) for n in range(8)]

        x = sb("x", [P, TILES, D])
        with ExitStack() as passing:
            def early(name, shape):
                return passing.enter_context(nc.sbuf_tensor(name, shape, F32R))

            hT_hi = early("hT_hi", [P, TILES, DC, P])
            hT_lo = early("hT_lo", [P, TILES, DC, P])
            early("below_pieces", [P, 3 * AC * T + TILES * 2 * GW])
            w_hi, w_lo = [None, None], [None, None]
            w_hi[0] = early("w0_hi", [P, DC, PIECE])
            w_lo[0] = [early(f"w0_lo{k}", [P, DC // 2, PIECE]) for k in range(2)]
            w_hi[1] = early("w1_hi", [P, DC, PIECE])
            w_lo[1] = [early("w1_lo0", [P, DC // 2, PIECE])]
            early("conv_rows", [P, CC * T])
            w_lo[1] += [early("w1_lo1", [P, DC // 2, PIECE])]
        wide = sb("wide", [P, TILES, DC, P])
        h_nat = sb("h_nat", [P, TILES, D])
        arena = sb("arena", [P, NBUF, 2 * D])
        diag = sb("diag", [P, NBUF, P])
        slabs = [sb(f"slab{n}", [P, DC * SLAB]) for n in range(NSLAB)]
        scores = sb("scores", [P, TILES, UNITS, KEYS])
        gain = sb("gain", [P, D])
        ident = sb("ident", [P, P])
        ident16 = sb("ident16", [P, P], BF16)
        causal = sb("causal", [P, P], BF16)
        zero16 = sb("zero16", [P, P], BF16)
        bsp = sb("bsp", [P, GG])
        mixg = sb("mixg", [P, DC])
        cw = sb("cw", [P, 3, CC])
        bf = sb("bf", [H, 1])
        ones = sb("ones", [P, 2])
        keysT = sb("keysT", [P, 2, KEYS])
        iota = sb("iota", [P, K])
        gate = sb("gate", [P, 2, SLOTS])
        eidx = sb("eidx", [P, 2, SLOTS], U32)
        stage = sb("stage", [P, NBUF], U32)
        gstage = sb("gstage", [P, BODY])
        dots = sb("dots", [P, BODY])
        gelu = sb("gelu", [P, BODY])
        wts = sb("wts", [P, BODY])
        stat = sb("stat", [P, 96])
        neghalf = sb("neghalf", [P, 16])

        flat = arena[:].rearrange("p a b -> p (a b)")

        def cut(region, at, shape):
            n = 1
            for s in shape:
                n *= s
            v = region[:, at:at + n]
            if len(shape) == 2:
                v = v.rearrange("p (a b) -> p a b", a=shape[0])
            return v, at + n

        at = 0
        qT, at = cut(flat, at, [AC, T])
        kT, at = cut(flat, at, [AC, T])
        v_nat, at = cut(flat, at, [TILES, AW])
        ug, at = cut(flat, at, [TILES, 2 * GW])
        negF, at = cut(flat, at, [H, T])
        mixT, at = cut(flat, at, [DC, T])
        assert at == NBUF * 2 * D
        TB = T - P
        qyA, _ = cut(gain[:], 0, [2, SLAB])
        sflat = scores[:].rearrange("p a b c -> p (a b c)")
        at = 0
        logit, at = cut(sflat, at, [DEEP, T])
        prob, at = cut(sflat, at, [DEEP, T])
        probT, at = cut(sflat, at, [2, T])
        o_att, at = cut(sflat, at, [2, AW])
        at = 0
        zpad, at = cut(sflat, at, [CC, T + 2])
        y_cv, at = cut(sflat, at, [CC, T])
        c_c, at = cut(sflat, at, [CC, T])
        vn, at = cut(sflat, at, [TILES, GW])
        zf, at = cut(sflat, at, [4, T])
        sgu_b, at = cut(sflat, at, [GW])
        wsp, at = cut(sflat, at, [GG, P])
        assert at <= TILES * UNITS * KEYS, at
        wflat = wide[:].rearrange("p a b c -> p (a b c)")
        qyB = [cut(region, n * TB, [TB])[0] for region in (gain[:], wflat) for n in range(2)]

        class Scratch:

            def __init__(self, small, cand, onehot):
                region, at = small
                self.vals, at = cut(region, at, [2 * HC, K])
                kidx, at = cut(region, at, [2 * HC, K])
                self.top, at = cut(region, at, [HC, K])
                tidx, at = cut(region, at, [HC, K])
                tsel, at = cut(region, at, [CS])
                self.tself, at = cut(region, at, [CS])
                self.epart, self.end = cut(region, at, [2, CS])
                self.cand, _ = cut(*cand, [K * K])
                self.onehot, _ = cut(*onehot, [CS * K])
                self.kidx, self.tidx, self.tsel = kidx.bitcast(U32), tidx.bitcast(U32), tsel.bitcast(U32)

        free_at = 2 * AC * T
        first_scratch = Scratch((sflat, (2 * UNITS - 4) * KEYS), (flat, free_at), (flat, free_at + K * K))
        later_scratch = Scratch((sflat, 0), (wflat, 2 * TB), (sflat, 2 * HC * KEYS))
        assert first_scratch.end <= 2 * UNITS * KEYS and later_scratch.end <= 2 * HC * KEYS
        assert CS * K <= 2 * HC * KEYS and 2 * TB + K * K <= D

        def scratch(t, c):
            return later_scratch if t or c else first_scratch

        def next_chunk(t, q):
            c = q // PC + 1
            return (t, c) if c < CHUNKS else (t + 1, 0)

        def chunk_no(l, t, c):
            return CHUNKS * (l * TILES + t) + c

        junk = wflat[:, 0:D]
        ss, ms, rstd = stat[:, 0:4], stat[:, 4:8], stat[:, 8:12]
        ssm = stat[:, 12:24]
        rm = stat[:, 24:36]
        rmax, nmax = stat[:, 84:87], stat[:, 87:90]
        rsum, rinv = stat[:, 90:93], stat[:, 93:96]
        gs, gr = stat[:, 44:60], stat[:, 60:76]
        dn = stat[:, 76:84]

        s_const = sem("const_loaded")
        s_layer = sem("layer_const_loaded")
        s_gain = sem("gain_loaded")
        s_setup = sem("setup_done")
        s_slab = [sem(f"slab{n}_loaded") for n in range(NSLAB)]
        full = [sem(f"bank{n}_full") for n in range(RING)]
        free = [sem(f"bank{n}_free") for n in range(RING)]
        s_vec = sem("vector_step")
        s_act = sem("scalar_step")
        s_sq = sem("square_summed")
        s_ms = sem("mean_square_ready")
        s_rms = sem("inverse_rms_ready")
        s_h = sem("h_ready")
        s_sp = sem("softplus_ready")
        s_hi = sem("weight_high_part_ready")
        s_lo = sem("weight_parts_ready")
        s_hT = sem("activation_high_part_ready")
        s_zf = sem("forget_logit_ready")
        s_F = sem("prefix_sums_ready")
        s_gelu = sem("gmlp_gelu_ready")
        s_vn = sem("gmlp_v_ready")
        s_og = sem("gmlp_out_ready")
        s_cv = sem("conv_out_ready")
        s_cvsq = sem("conv_squares_ready")
        s_nmax = sem("row_max_ready")
        s_exp = sem("prob_ready")
        s_pv = sem("head_out_in_psum")
        s_oh = sem("head_out_ready")
        s_x = sem("x_mixed")
        s_sc = sem("exp_scores_ready")
        s_idx = sem("expert_numbers_ready")
        s_gates = sem("gates_ready")
        s_gexp = sem("gate_logits_ready")
        s_stage = sem("index_staged")
        s_land = [sem(f"slot_landed{n}") for n in range(NBUF)]
        s_dot = sem("dot_ready")
        s_ge = sem("expert_gelu_ready")
        s_w = sem("expert_weight_ready")
        s_dg = sem("diag_ready")
        s_used = sem("slots_free")
        s_acc = sem("experts_summed")
        s_xe = sem("x_with_experts")
        s_out = sem("final_ready")
        s_st = sem("stored")

        def wait_full(eng, l, *key):
            n = turn(l, *key)
            eng.wait_ge(full[n % RING], n // RING + 1)
            return banks[n % RING]

        def wait_free(eng, l, *key):
            n = turn(l, *key)
            if n >= RING:
                eng.wait_ge(free[n % RING], n // RING)
            return banks[n % RING]

        def is_full(ins, l, *key):
            ins.then_inc(full[turn(l, *key) % RING], 1)

        def is_free(ins, l, *key):
            ins.then_inc(free[turn(l, *key) % RING], 1)

        last_turn = [None] * N_IN
        last_turn += [("OC", f, TILES - 1) for f in range(N_OUT)]
        last_turn += [("QA", 0)] + [("QB", (f + 1) * (SLAB // P) - 1) for f in range(NQ)]
        rms_of_layer = [rstd, gr, rm] + [rstd[:, i:i + 1] for i in range(TILES)]
        RMS = len(rms_of_layer)

        def acc_banks(t):
            return banks[6:8] if t % 2 == 0 else banks[4:6]

        def slab_no(l, s):
            return l * SLABS + s

        def slab_view(l, s, cols=SLAB):
            return slabs[slab_no(l, s) % NSLAB][:, 0:DC * cols].rearrange("p (c n) -> p c n", c=DC)

        def wait_slab(eng, l, s):
            n = slab_no(l, s)
            loads = sum(2 if m % SLABS == 0 else 1 for m in range(n % NSLAB, n + 1, NSLAB))
            eng.wait_ge(s_slab[n % NSLAB], 16 * loads)

        def raw(l, p):
            s, c0, cols, _ = pieces[p]
            return slab_view(l, s, H + CW if s == S_F else SLAB)[:, :, c0:c0 + cols]

        block = ctx.enter_context(nc.Block())

        @block.sync
        def _(sp):
            sp.dma_start(x[:], x_d.rearrange("(i p) d -> p i d", p=P)).then_inc(s_const, 16)
            for l in range(L):
                def parameters():
                    if l:
                        sp.wait_ge(s_xe, l * TILES)
                    sp.dma_start(gain[:], norm1_g[l:l + 1, :].broadcast_to([P, D])).then_inc(s_gain, 16)
                    sp.dma_start(sgu_b[:], sgu_g[l:l + 1, :].broadcast_to([P, GW])).then_inc(s_layer, 16)
                    sp.dma_start(wsp[:], w_spatial[l]).then_inc(s_layer, 16)
                    sp.dma_start(bsp[:], b_spatial[l]).then_inc(s_layer, 16)
                    sp.dma_start(mixg[:], mix_g[l]).then_inc(s_layer, 16)
                    sp.dma_start(cw[:], conv_w[l]).then_inc(s_layer, 16)
                    sp.dma_start(bf[:], b_forget[l].unsqueeze(1)).then_inc(s_layer, 16)
                    sp.dma_start(keysT[:], sub_keys[l]).then_inc(s_layer, 16)

                if l == 0:
                    parameters()
                for s in range(SLABS):
                    if l and s == NSLAB:
                        parameters()
                    n = slab_no(l, s)
                    if n >= NSLAB:
                        before, b = (n - NSLAB) // SLABS, (n - NSLAB) % SLABS
                        if b < N_IN:
                            sp.wait_ge(s_lo, before * NP + max(p for p in range(NP) if pieces[p][0] == b) + 1)
                        else:
                            m = turn(before, *last_turn[b])
                            sp.wait_ge(free[m % RING], m // RING + 1)
                    arrived = s_slab[n % NSLAB]
                    if s == S_F:
                        dst = slab_view(l, s, H + CW)
                        sp.dma_start(dst[:, :, 0:H], w_in[l, :, :, O_F:O_F + H]).then_inc(arrived, 16)
                        sp.dma_start(dst[:, :, H:H + CW],
                                     w_in[l, :, :, O_C + 2 * CW:O_C + 3 * CW]).then_inc(arrived, 16)
                    elif s < N_IN:
                        o = {S_C: O_C, S_G: O_G, S_V: O_V, S_Q: O_Q, S_K: O_K}[s]
                        sp.dma_start(slab_view(l, s), w_in[l, :, :, o:o + SLAB]).then_inc(arrived, 16)
                    elif s < S_QY:
                        o = (s - S_O) * SLAB
                        sp.dma_start(slab_view(l, s), w_out[l, :, :, o:o + SLAB]).then_inc(arrived, 16)
                    else:
                        o = (s - S_QY) % NQ * SLAB
                        sp.dma_start(slab_view(l, s), w_query[l, :, :, o:o + SLAB]).then_inc(arrived, 16)
                    if s == S_O:
                        sp.wait_ge(s_h, 2 * l * TILES + TILES)
                        sp.dma_start(gain[:], norm2_g[l:l + 1, :].broadcast_to([P, D])).then_inc(s_gain, 16)
            sp.wait_ge(s_acc, (L - 1) * TILES + 1)
            sp.dma_start(gain[:], final_g.rearrange("(a d) -> a d", a=1).broadcast_to([P, D]))\
              .then_inc(s_gain, 16)
            for i in range(TILES):
                sp.wait_ge(s_out, i + 1)
                sp.dma_start(out_d[i * P:(i + 1) * P, :], h_nat[:, i, :]).then_inc(s_st, 16)
            sp.wait_ge(s_st, 16 * TILES)

        @block.gpsimd
        def _(pool):
            nc.gpsimd.memset(ident[:], 0.0).then_inc(s_setup, 1)
            nc.gpsimd.memset(causal[:], 0.0).then_inc(s_setup, 1)
            nc.gpsimd.memset(zero16[:], 0.0).then_inc(s_setup, 1)
            nc.gpsimd.memset(ones[:], 1.0).then_inc(s_setup, 1)
            nc.gpsimd.memset(neghalf[:], -0.5).then_inc(s_setup, 1)
            nc.gpsimd.iota(iota[:], pattern=[[1, K]], base=0, channel_multiplier=0,
                           allow_small_or_imprecise_dtypes=True).then_inc(s_setup, 1)
            pool.wait_ge(s_setup, 6)
            nc.gpsimd.affine_select(out=ident[:], in_=ident[:], compare_op=ALU.not_equal, fill=1.0, base=0,
                                    pattern=[[-1, P]], channel_multiplier=1).then_inc(s_setup, 1)
            nc.gpsimd.affine_select(out=causal[:], in_=causal[:], compare_op=ALU.is_ge, fill=MASKED / SCALE,
                                    base=0, pattern=[[-1, P]], channel_multiplier=1).then_inc(s_setup, 1)
            pool.wait_ge(s_setup, 8)
            nc.gpsimd.tensor_copy(ident16[:], ident[:]).then_inc(s_setup, 1)
            def inverse_roots(n, dst):
                pool.wait_ge(s_ms, n + 1)
                nc.gpsimd.tensor_tensor(dst, dst, neghalf[:, 0:dst.shape[1]], ALU.pow).then_inc(s_rms, 1)

            def gather_chunk(n0, t, c0):
                with pool.Fori(0, CS // BODY) as it:
                    for b in range(BODY):
                        j = b % NBUF
                        pool.wait_ge(s_used, it * BODY + (n0 + b + 1))
                        pool.nop(nofuse=True)
                        nc.gpsimd.tensor_copy(stage[:, j:j + 1],
                                              eidx[:, t % 2, bass.ds(it * BODY + (c0 + b), 1)])\
                          .then_inc(s_stage, 1)
                        pool.wait_ge(s_stage, it * BODY + (n0 + b + 1))
                        pool.nop(nofuse=True)
                        nc.gpsimd.indirect_dma_start(
                            arena[:, j, :], None, uv,
                            bass.IndirectOffsetOnAxis(ap=stage[:, j:j + 1], axis=0)).then_inc(s_land[j], 16)

            for l in range(L):
                pool.wait_ge(s_layer, 16 * 7 * (l + 1))
                nc.gpsimd.affine_select(out=wsp[:], in_=wsp[:], compare_op=ALU.is_ge, fill=0.0, base=0,
                                        pattern=[[0, GG], [1, P]], channel_multiplier=-1).then_inc(s_setup, 1)
                for k, dst in enumerate(rms_of_layer):
                    inverse_roots(l * RMS + k, dst)
                for t in range(TILES):
                    n0 = (l * TILES + t) * SLOTS
                    for c in range(CHUNKS):
                        pool.wait_ge(s_idx, chunk_no(l, t, c) + 1)
                        gather_chunk(n0 + c * CS, t, c * CS)
            inverse_roots(L * RMS, rstd)

        @block.scalar
        def _(act):
            steps = [0]

            def step(ins):
                steps[0] += 1
                ins.then_inc(s_act, 1)
                act.wait_ge(s_act, steps[0])

            def copy_out(dst, l, *key, scale=1.0):
                b = wait_full(act, l, *key)
                n = 1
                for s in dst.shape[1:]:
                    n *= s
                is_free(nc.scalar.activation(dst, b[0:dst.shape[0], 0:n].rearrange("p (a b) -> p a b", a=dst.shape[1])
                                             if len(dst.shape) == 3 else b[0:dst.shape[0], 0:n],
                                             ACT.Copy, scale=scale), l, *key)

            squared = [0]

            def square(src, total):
                if squared[0]:
                    act.wait_ge(s_sq, squared[0])
                squared[0] += 1
                nc.scalar.activation(junk[:, 0:src.shape[1]], src, ACT.Square, accum_out=total).then_inc(s_sq, 1)

            act.wait_ge(s_const, 16)
            for l in range(L):
                if l:
                    act.wait_ge(s_xe, l * TILES)
                for i in range(TILES):
                    square(x[:, i, :], ss[:, i:i + 1])
                def split(p):
                    if p >= 2:
                        wait_full(act, l, *pieces[p - 2][3])
                    if p == 0 or pieces[p][0] != pieces[p - 1][0]:
                        wait_slab(act, l, pieces[p][0])
                    nc.scalar.activation(w_hi[p % 2][:, :, 0:pieces[p][2]], raw(l, p), ACT.Copy).then_inc(s_hi, 1)

                split(0)
                split(1)
                for i in range(TILES):
                    for f in range(2):
                        b = wait_full(act, l, "T1", i, f)
                        nc.scalar.activation(hT_hi[:, i, f * (DC // 2):(f + 1) * (DC // 2), :],
                                             b[:].rearrange("p (c n) -> p c n", c=DC // 2), ACT.Copy)\
                          .then_inc(s_hT, 1)
                split(2)
                act.wait_ge(s_zf, l + 1)
                step(nc.scalar.activation(zf[0:H, 1, :], zf[0:H, 1, :], ACT.Exp))
                nc.scalar.activation(zf[0:H, 1, :], zf[0:H, 1, :], ACT.Ln, bias=1.0).then_inc(s_sp, 1)
                for c in range(CC):
                    copy_out(c_c[:, c, :], l, "CC", c)
                for p in range(3, 6):
                    split(p)
                for f in range(2):
                    for i in range(TILES):
                        b = wait_full(act, l, "G", f, i)
                        nc.scalar.activation(ug[:, i, f * GW:(f + 1) * GW], b[:, 0:GW], ACT.Gelu_apprx_tanh)\
                          .then_inc(free[turn(l, "G", f, i) % RING], 1)
                    split(6 + f)
                    if f == 0:
                        for c in range(CC):
                            act.wait_ge(s_cv, l * CC + c + 1)
                            nc.scalar.activation(c_c[:, c, :], y_cv[:, c, :], ACT.Square).then_inc(s_cvsq, 1)
                for f in range(2):
                    for i in range(TILES):
                        copy_out(v_nat[:, i, f * PIECE:(f + 1) * PIECE], l, "V", f, i)
                    split(8 + f)
                split(10)
                split(11)
                for c in range(AC):
                    copy_out(kT[:, c, :], l, "K", c)
                for h in range(0, H, 2):
                    copy_out(negF[:, h, :], l, "FB", h, scale=-1.0 / SCALE)
                for i in range(TILES):
                    act.wait_ge(s_og, l * TILES + i + 1)
                    square(ug[:, i, 0:GW], ssm[:, 4 + i:5 + i])
                for s in range(UN + O_LAG):
                    if s < UN:
                        d, W = s % DEEP, (s // H + 1) * P
                        act.wait_ge(s_nmax, l * UN + s + 1)
                        nc.scalar.activation(prob[:, d, 0:W], logit[:, d, 0:W], ACT.Exp, bias=nmax[:, d:d + 1],
                                             accum_out=rsum[:, d:d + 1]).then_inc(s_exp, 1)
                    if T_LAG <= s < UN + T_LAG:
                        v = s - T_LAG
                        copy_out(probT[:, v % 2, 0:(v // H + 1) * P], l, "P", v)
                    if s >= O_LAG and (s - O_LAG) % H == H - 1:
                        act.wait_ge(s_oh, l * UN + s - O_LAG + 1)
                        i = (s - O_LAG) // H
                        square(o_att[:, i % 2, :], ssm[:, i:i + 1])
                for i in range(TILES):
                    act.wait_ge(s_x, l * TILES + i + 1)
                    square(x[:, i, :], ss[:, i:i + 1])
                def gate_exp(t, c):
                    act.wait_ge(s_gexp, chunk_no(l, t, c) + 1)
                    top = scratch(t, c).top
                    nc.scalar.activation(top, top, ACT.Exp).then_inc(s_sc, 1)

                act.wait_ge(s_sq, squared[0])
                for i in range(2):
                    copy_out(wide[:, i, 0:DC // 2, :], l, "T2", i, 0)
                act.wait_ge(s_h, (2 * l + 2) * TILES)
                copy_out(qyA[:, 0, :], l, "QA", 0)
                for i in range(2, TILES):
                    copy_out(wide[:, i, 0:DC // 2, :], l, "T2", i, 0)
                for c in range(1, NQ):
                    copy_out(qyA[:, c % 2, :], l, "QA", c)
                    if c >= 2:
                        copy_out(scores[:, 0, 4 * c - 4:4 * c, :], l, "SA", c - 1)
                    if c == 2:
                        gate_exp(0, 0)
                copy_out(qyB[0], l, "QB", 0)
                copy_out(scores[:, 0, UNITS - 4:UNITS, :], l, "SA", NQ - 1)
                for c in range(1, EARLY):
                    copy_out(qyB[c % 4], l, "QB", c)
                    copy_out(scores[:, 1:TILES, c - 1, :], l, "SB", c - 1)
                copy_out(scores[:, 1:TILES, EARLY - 1, :], l, "SB", EARLY - 1)
                for t in range(TILES):
                    for q in range(PARTS):
                        if t == 0:
                            for c in late(q - 1):
                                copy_out(qyB[c % 4], l, "QB", c)
                        if q % PC == PC - 1 and chunk_no(0, t, q // PC) + 1 < CHUNKS * TILES:
                            gate_exp(*next_chunk(t, q))
                        if q % PC == 0:
                            act.wait_ge(s_gates, chunk_no(l, t, q // PC) + 1)
                        c0 = q * LOOP * BODY
                        n0 = (l * TILES + t) * SLOTS + c0
                        with act.Fori(0, LOOP) as it:
                            nc.scalar.activation(gstage[:], gate[:, t % 2, bass.ds(it * BODY + c0, BODY)], ACT.Copy)
                            for b in range(0, BODY, GROUP):
                                group = slice(b, b + GROUP)
                                done = n0 + b + GROUP
                                act.wait_ge(s_dot, it * BODY + done)
                                nc.scalar.activation(gelu[:, group], dots[:, group], ACT.Gelu_apprx_tanh)\
                                  .then_inc(s_ge, GROUP)
                                act.wait_ge(s_ge, it * BODY + done)
                                for k in range(b, b + GROUP):
                                    nc.scalar.activation(wts[:, k:k + 1], gelu[:, k:k + 1], ACT.Copy,
                                                         scale=gstage[:, k:k + 1]).then_inc(s_w, 1)
                                act.wait_ge(s_w, it * BODY + done)
                                for k in range(b, b + GROUP):
                                    act.wait_ge(s_used, it * BODY + (n0 + k + 1))
                                    nc.scalar.activation(diag[:, k % NBUF, :], ident[:], ACT.Copy,
                                                         scale=wts[:, k:k + 1]).then_inc(s_dg, 1)
            for i in range(TILES):
                act.wait_ge(s_xe, (L - 1) * TILES + i + 1)
                square(x[:, i, :], ss[:, i:i + 1])

        @block.vector
        def _(dve):
            V = nc.vector
            steps = [0]
            squares = [0]

            def step(ins):
                steps[0] += 1
                ins.then_inc(s_vec, 1)
                dve.wait_ge(s_vec, steps[0])

            def copy_out(dst, l, *key):
                b = wait_full(dve, l, *key)
                n = 1
                for s in dst.shape[1:]:
                    n *= s
                src = b[:, 0:n].rearrange("p (a b) -> p a b", a=dst.shape[1]) if len(dst.shape) == 3 else b[:, 0:n]
                is_free(V.tensor_copy(dst, src), l, *key)

            roots = [0]

            def mean_square(dst, src, width):
                return V.tensor_scalar(dst, src, 1.0 / width, EPS, ALU.mult, ALU.add)

            def wait_roots(ins):
                ins.then_inc(s_ms, 1)
                roots[0] += 1
                dve.wait_ge(s_rms, roots[0])

            def norm_scales():
                squares[0] += TILES
                dve.wait_ge(s_sq, squares[0])
                wait_roots(mean_square(rstd, ss, D))

            def norm(i):
                return V.scalar_tensor_tensor(out=h_nat[:, i, :], in0=x[:, i, :], scalar=rstd[:, i:i + 1],
                                              in1=gain[:], op0=ALU.mult, op1=ALU.mult)

            def topk_head(l, t, h):
                w, k = scratch(t, h // HC), h % HC
                if t < 2:
                    for key in (("SA", 2 * h // 4),) if t == 0 else (("SB", 2 * h), ("SB", 2 * h + 1)):
                        n = turn(l, *key)
                        dve.wait_ge(free[n % RING], n // RING + 1)
                for half in range(2):
                    s, v, n = scores[:, t, 2 * h + half, :], w.vals[:, 2 * k + half, :], w.kidx[:, 2 * k + half, :]
                    step(V.max(v[:, 0:8], s))
                    V.max_index(n[:, 0:8], v[:, 0:8], s)
                    step(V.match_replace(s, v[:, 0:8], s, NEG))
                    step(V.max(v[:, 8:16], s))
                    step(V.max_index(n[:, 8:16], v[:, 8:16], s))
                s, v, n = w.cand, w.top[:, k, :], w.tidx[:, k, :]
                step(V.tensor_tensor(s.rearrange("p (a b) -> p a b", a=K),
                                     w.vals[:, 2 * k, :].unsqueeze(2).broadcast_to([P, K, K]),
                                     w.vals[:, 2 * k + 1, :].unsqueeze(1).broadcast_to([P, K, K]), ALU.add))
                step(V.max(v[:, 0:8], s))
                V.max_index(n[:, 0:8], v[:, 0:8], s)
                step(V.match_replace(s, v[:, 0:8], s, NEG))
                step(V.max(v[:, 8:16], s))
                step(V.max_index(n[:, 8:16], v[:, 8:16], s))

            def gate_logits(t, c):
                w = scratch(t, c)
                step(V.tensor_copy(dn[:, 0:HC], w.top[:, :, 0]))
                V.tensor_tensor(w.top, w.top, dn[:, 0:HC].unsqueeze(2).broadcast_to([P, HC, K]),
                                ALU.subtract).then_inc(s_gexp, 1)

            def expert_numbers(l, t, c):
                w = scratch(t, c)
                places = w.tidx.rearrange("p h k -> p (h k)")
                oh = w.onehot.rearrange("p (a b) -> p a b", b=K)
                oh4 = w.onehot.rearrange("p (h a b) -> p h a b", h=HC, b=K)
                for half in range(2):
                    if half == 0:
                        step(V.tensor_scalar(w.tsel, places, 4, None, ALU.logical_shift_right))
                    else:
                        step(V.tensor_scalar(w.tsel, places, 15, None, ALU.bitwise_and))
                    V.tensor_copy(w.tself, w.tsel)
                    ep = w.epart[:, half, :]
                    ep3 = ep.rearrange("p (h k) -> p h k", h=HC)
                    step(V.tensor_copy(ep3, w.kidx.rearrange("p (h f) k -> p h f k", f=2)[:, :, half, :]))
                    step(V.tensor_tensor(oh, iota[:].unsqueeze(1).broadcast_to([P, CS, K]),
                                         w.tself.unsqueeze(2).broadcast_to([P, CS, K]), ALU.is_equal))
                    step(V.tensor_tensor(oh4, oh4, ep3.unsqueeze(2).broadcast_to([P, HC, K, K]), ALU.mult))
                    step(V.tensor_reduce(ep, oh, AX.X, ALU.add))
                step(V.scalar_tensor_tensor(out=w.epart[:, 0, :], in0=w.epart[:, 0, :], scalar=float(KEYS),
                                            in1=w.epart[:, 1, :], op0=ALU.mult, op1=ALU.add))
                step(V.tensor_scalar(w.epart[:, 0, :], w.epart[:, 0, :], float(l * NE), None, ALU.add))
                V.tensor_copy(eidx[:, t % 2, c * CS:(c + 1) * CS], w.epart[:, 0, :]).then_inc(s_idx, 1)
                dve.wait_ge(s_idx, chunk_no(l, t, c) + 1)

            def gates(l, t, c):
                w = scratch(t, c)
                dve.wait_ge(s_sc, chunk_no(l, t, c) + 1)
                step(V.tensor_reduce(dn[:, 0:HC], w.top, AX.X, ALU.add))
                step(V.reciprocal(dn[:, 0:HC], dn[:, 0:HC]))
                V.tensor_tensor(gate[:, t % 2, c * CS:(c + 1) * CS].rearrange("p (h k) -> p h k", h=HC), w.top,
                                dn[:, 0:HC].unsqueeze(2).broadcast_to([P, HC, K]), ALU.mult).then_inc(s_gates, 1)

            def routing_part(l, t, q):
                t, c = next_chunk(t, q)
                if t < TILES:
                    if q % PC == 0:
                        for k in range(HC):
                            topk_head(l, t, c * HC + k)
                        gate_logits(t, c)
                    if q % PC == PC - 1:
                        expert_numbers(l, t, c)
                        gates(l, t, c)

            def add_experts(l, t):
                dve.wait_ge(s_acc, l * TILES + t + 1)
                for f in range(2):
                    xs = x[:, t, f * 512:(f + 1) * 512]
                    ins = V.tensor_tensor(xs, acc_banks(t)[f][:], xs, ALU.add)
                ins.then_inc(s_xe, 1)

            dve.wait_ge(s_const, 16)
            for l in range(L):
                dve.wait_ge(s_gain, 16 * (2 * l + 1))
                dve.wait_ge(s_layer, 16 * 7 * (l + 1))
                def split(p):
                    w, cols = raw(l, p), pieces[p][2]
                    dve.wait_ge(s_hi, l * NP + p + 1)
                    for k, lo in enumerate(w_lo[p % 2]):
                        half = slice(k * (DC // 2), (k + 1) * (DC // 2))
                        ins = V.tensor_tensor(lo[:, :, 0:cols], w[:, half, :],
                                              w_hi[p % 2][:, half, 0:cols].bitcast(F32), ALU.subtract)
                    ins.then_inc(s_lo, 1)

                def split_activations(i):
                    for f in range(2):
                        half = slice(f * (DC // 2), (f + 1) * (DC // 2))
                        b = wait_full(dve, l, "T1", i, f)
                        dve.wait_ge(s_hT, (l * TILES + i) * 2 + f + 1)
                        is_free(V.tensor_tensor(hT_lo[:, i, half, :], b[:].rearrange("p (c n) -> p c n", c=DC // 2),
                                                hT_hi[:, i, half, :].bitcast(F32), ALU.subtract), l, "T1", i, f)

                norm_scales()
                for i in range(TILES):
                    norm(i).then_inc(s_h, 1)
                    if i:
                        split_activations(i - 1)
                split(0)
                split_activations(TILES - 1)
                split(1)
                b = wait_full(dve, l, "ZF")
                for c in range(CC):
                    V.memset(zpad[:, c, 0:2], 0.0)
                is_free(V.tensor_scalar(zf[0:H, 0, :], b[0:H, :], bf[:, 0:1], None, ALU.add), l, "ZF")
                dve.wait_ge(free[turn(l, "ZF") % RING], turn(l, "ZF") // RING + 1)
                V.scalar_tensor_tensor(out=zf[0:H, 1, :], in0=zf[0:H, 0, :], scalar=-1.0, in1=zf[0:H, 0, :],
                                       op0=ALU.mult, op1=ALU.min).then_inc(s_zf, 1)
                split(2)
                split(3)
                for c in range(CC):
                    b = wait_full(dve, l, "CI", c)
                    if c == 0:
                        for k in range(CC):
                            n = turn(l, "CC", k)
                            dve.wait_ge(free[n % RING], n // RING + 1)
                    is_free(V.tensor_tensor(zpad[:, c, 2:T + 2], b[:], c_c[:, c, :], ALU.mult), l, "CI", c)
                split(4)
                for c in range(CC):
                    n = turn(l, "CI", c)
                    dve.wait_ge(free[n % RING], n // RING + 1)
                    y = y_cv[:, c, :]
                    step(V.tensor_scalar(y, zpad[:, c, 0:T], cw[:, 0, c:c + 1], None, ALU.mult))
                    step(V.scalar_tensor_tensor(out=y, in0=zpad[:, c, 1:T + 1], scalar=cw[:, 1, c:c + 1], in1=y,
                                                op0=ALU.mult, op1=ALU.add))
                    step(V.scalar_tensor_tensor(out=y, in0=zpad[:, c, 2:T + 2], scalar=cw[:, 2, c:c + 1], in1=y,
                                                op0=ALU.mult, op1=ALU.add))
                    b = wait_full(dve, l, "CB", c)
                    is_free(V.tensor_tensor(y, b[:], y, ALU.mult), l, "CB", c)
                    n = turn(l, "CB", c)
                    dve.wait_ge(free[n % RING], n // RING + 1)
                    V.tensor_scalar(mixT[:, AC + GC + c, :], y, mixg[:, AC + GC + c:AC + GC + c + 1], None,
                                    ALU.mult).then_inc(s_cv, 1)
                split(5)
                dve.wait_ge(s_sp, l + 1)
                step(V.scalar_tensor_tensor(out=zf[0:H, 2, :], in0=zf[0:H, 0, :], scalar=0.0, in1=zf[0:H, 1, :],
                                            op0=ALU.min, op1=ALU.subtract))
                step(V.memset(zf[0:H, 0, :], 1.0))
                V.tensor_tensor_scan(zf[0:H, 3, :], zf[0:H, 0, :], zf[0:H, 2, :], 0.0, ALU.mult, ALU.add)\
                 .then_inc(s_F, 1)
                split(6)
                for i in range(TILES):
                    n = turn(l, "G", 1, i)
                    dve.wait_ge(free[n % RING], n // RING + 1)
                    gv = ug[:, i, GW:2 * GW]
                    step(V.tensor_tensor(vn[:, i, :], gv, gv, ALU.mult))
                    step(V.tensor_reduce(gs[:, i * GG:(i + 1) * GG], vn[:, i, :].rearrange("p (g d) -> p g d", g=GG),
                                         AX.X, ALU.add))
                split(7)
                wait_roots(mean_square(gr, gs, GD))
                for i in range(TILES):
                    vi = vn[:, i, :]
                    step(V.tensor_tensor(vi.rearrange("p (g d) -> p g d", g=GG),
                                         ug[:, i, GW:2 * GW].rearrange("p (g d) -> p g d", g=GG),
                                         gr[:, i * GG:(i + 1) * GG].unsqueeze(2).broadcast_to([P, GG, GD]), ALU.mult))
                    V.tensor_tensor(vi, vi, sgu_b[:], ALU.mult).then_inc(s_vn, 1)
                split(8)
                split(9)
                for c in range(AC):
                    copy_out(qT[:, c, :], l, "Q", c)
                    if c % 2:
                        split(10 + c // 2)
                for h in range(1, H, 2):
                    b = wait_full(dve, l, "FB", h)
                    is_free(V.tensor_scalar(negF[:, h, :], b[:], -1.0 / SCALE, None, ALU.mult), l, "FB", h)
                for i in range(TILES):
                    b = wait_full(dve, l, "GM", i)
                    for g in range(GG):
                        sl = slice(g * GD, (g + 1) * GD)
                        ins = V.scalar_tensor_tensor(out=ug[:, i, sl], in0=b[:, sl], scalar=bsp[:, g:g + 1],
                                                     in1=ug[:, i, sl], op0=ALU.add, op1=ALU.mult)
                    is_free(ins, l, "GM", i)
                    n = turn(l, "GM", i)
                    dve.wait_ge(free[n % RING], n // RING + 1)
                    dve.nop().then_inc(s_og, 1)
                b = wait_full(dve, l, "CS")
                is_free(V.tensor_copy(ssm[:, 8:8 + TILES], b[:, 0:TILES]), l, "CS")
                for i in range(TILES):
                    b = wait_full(dve, l, "GT", i)
                    is_free(V.tensor_tensor(mixT[:, AC:AC + GC, i * P:(i + 1) * P],
                                            b[:, 0:GC * P].rearrange("p (c n) -> p c n", c=GC),
                                            mixg[:, AC:AC + GC].unsqueeze(2).broadcast_to([P, GC, P]), ALU.mult),
                            l, "GT", i)
                for h in range(0, H, 2):
                    n = turn(l, "FB", h)
                    dve.wait_ge(free[n % RING], n // RING + 1)
                for s in range(UN + AT_LAG):
                    if s < UN:
                        h, d, W = s % H, s % DEEP, (s // H + 1) * P
                        b = wait_full(dve, l, "S", s)
                        if s >= DEEP:
                            dve.wait_ge(s_exp, l * UN + s - DEEP + 1)
                        is_free(V.tensor_tensor_reduce(out=logit[:, d, 0:W], in0=b[:, 0:W], in1=negF[:, h, 0:W],
                                                       scale=SCALE, scalar=-3.0e38, op0=ALU.add, op1=ALU.max,
                                                       accum_out=rmax[:, d:d + 1]), l, "S", s)
                        n = turn(l, "S", s)
                        dve.wait_ge(free[n % RING], n // RING + 1)
                        V.tensor_scalar(nmax[:, d:d + 1], rmax[:, d:d + 1], -1.0, None, ALU.mult).then_inc(s_nmax, 1)
                    if O_LAG <= s < UN + O_LAG:
                        w = s - O_LAG
                        i, h = w // H, w % H
                        dve.wait_ge(s_pv, l * UN + w + 1)
                        if w >= 2 * H and h == 0:
                            dve.wait_ge(s_sq, squares[0] + TILES + (i - 2) + 1)
                        V.tensor_scalar(o_att[:, i % 2, h * DH:(h + 1) * DH], banks[6 + w % 2][:, 0:DH],
                                        rinv[:, w % DEEP:w % DEEP + 1], None, ALU.mult).then_inc(s_oh, 1)
                    if T_LAG <= s < UN + T_LAG:
                        w = s - T_LAG
                        dve.wait_ge(s_exp, l * UN + w + 1)
                        step(V.reciprocal(rinv[:, w % DEEP:w % DEEP + 1], rsum[:, w % DEEP:w % DEEP + 1]))
                    if s >= AT_LAG and (s - AT_LAG) % H == H - 1:
                        i = (s - AT_LAG) // H
                        b = wait_full(dve, l, "AT", i)
                        is_free(V.tensor_tensor(mixT[:, 0:AC, i * P:(i + 1) * P],
                                                b[:].rearrange("p (c n) -> p c n", c=AC),
                                                mixg[:, 0:AC].unsqueeze(2).broadcast_to([P, AC, P]), ALU.mult),
                                l, "AT", i)
                def mean_square_2(i):
                    dve.wait_ge(s_sq, squares[0] + i + 1)
                    mean_square(rstd[:, i:i + 1], ss[:, i:i + 1], D).then_inc(s_ms, 1)

                def norm_2(i):
                    if i == 0:
                        dve.wait_ge(s_gain, 16 * (2 * l + 2))
                    roots[0] += 1
                    dve.wait_ge(s_rms, roots[0])
                    norm(i).then_inc(s_h, 1)

                squares[0] += 2 * TILES
                dve.wait_ge(s_sq, squares[0])
                n = turn(l, "CS")
                dve.wait_ge(free[n % RING], n // RING + 1)
                step(mean_square(rm[:, 0:4], ssm[:, 0:4], AW))
                step(mean_square(rm[:, 4:8], ssm[:, 4:8], GW))
                wait_roots(mean_square(rm[:, 8:12], ssm[:, 8:12], CW))
                for f in range(N_OUT):
                    for i in range(TILES):
                        xs = x[:, i, f * SLAB:(f + 1) * SLAB]
                        for k, key in enumerate(("OA", "OG", "OC")):
                            b = wait_full(dve, l, key, f, i)
                            ins = V.scalar_tensor_tensor(out=xs, in0=b[:], scalar=rm[:, 4 * k + i:4 * k + i + 1], in1=xs,
                                                         op0=ALU.mult, op1=ALU.add)
                            is_free(ins, l, key, f, i)
                            n = turn(l, key, f, i)
                            dve.wait_ge(free[n % RING], n // RING + 1)
                        if f == N_OUT - 1:
                            dve.nop().then_inc(s_x, 1)
                            if i >= 2:
                                norm_2(i - 2)
                            if i >= 1:
                                mean_square_2(i - 1)
                norm_2(TILES - 2)
                mean_square_2(TILES - 1)
                copy_out(wide[:, 0, DC // 2:DC, :], l, "T2", 0, 1)
                norm_2(TILES - 1)
                for i in range(1, TILES):
                    copy_out(wide[:, i, DC // 2:DC, :], l, "T2", i, 1)
                copy_out(scores[:, 0, 0:4, :], l, "SA", 0)
                for k in range(HC):
                    topk_head(l, 0, k)
                gate_logits(0, 0)
                expert_numbers(l, 0, 0)
                gates(l, 0, 0)
                n = turn(l, "SA", NQ - 1)
                dve.wait_ge(free[n % RING], n // RING + 1)
                squares[0] += TILES
                for t in range(TILES):
                    for q in range(PARTS):
                        n0 = (l * TILES + t) * SLOTS + q * LOOP * BODY
                        if t * PARTS + q <= PARTS:
                            for c in late(t * PARTS + q - 2):
                                copy_out(scores[:, 1:TILES, c, :], l, "SB", c)
                        routing_part(l, t, q)
                        with dve.Fori(0, LOOP) as it:
                            for b in range(BODY):
                                dve.wait_ge(s_land[b % NBUF], it * (16 * BODY // NBUF) + 16 * ((n0 + b) // NBUF + 1))
                                uu = arena[:, b % NBUF, 0:D]
                                V.tensor_tensor_reduce(out=uu, in0=uu, in1=h_nat[:, t, :], scale=1.0, scalar=0.0,
                                                       op0=ALU.mult, op1=ALU.add,
                                                       accum_out=dots[:, b:b + 1])\
                                 .then_inc(s_dot, 1)
                        if q == 0 and t:
                            add_experts(l, t - 1)
                add_experts(l, TILES - 1)
                dve.wait_ge(s_xe, (l + 1) * TILES)
            dve.wait_ge(s_gain, 16 * (2 * L + 1))
            norm_scales()
            for i in range(TILES):
                norm(i).then_inc(s_out, 1)

        @block.tensor
        def _(pe):
            def mm(out, lhsT, rhs, start, stop):
                return nc.tensor.matmul(out, lhsT, rhs, start=start, stop=stop)

            def transposes(l, i, name, f):
                b = wait_free(pe, l, name, i, f)
                for c in range(DC // 2):
                    col = (f * (DC // 2) + c) * P
                    ins = nc.tensor.transpose(b[:, c * P:(c + 1) * P], h_nat[:, i, col:col + P], ident[:])
                is_full(ins, l, name, i, f)

            def products(out, l, p, c0, cols, tile=None):
                for c in range(DC):
                    hi = w_hi[p % 2][:, c, c0:c0 + cols]
                    lo = w_lo[p % 2][c // (DC // 2)][:, c % (DC // 2), c0:c0 + cols]
                    for k, (w, h) in enumerate(((hi, hT_hi), (lo, hT_hi), (hi, hT_lo))):
                        first, last = c == 0 and k == 0, c == DC - 1 and k == 2
                        if tile is None:
                            ins = mm(out, w, h[:, :, c, :], first, last)
                        else:
                            ins = mm(out, h[:, tile, c, :], w, first, last)
                return ins

            def feature_major(l, p, c0, *key):
                b = wait_free(pe, l, *key)
                is_full(products(b[:], l, p, c0, P), l, *key)

            def token_major(l, p, i, *key):
                b = wait_free(pe, l, *key)
                is_full(products(b[:, 0:PIECE], l, p, 0, PIECE, i), l, *key)

            def wait_piece(l, p):
                pe.wait_ge(s_lo, l * NP + p + 1)

            def zeros(bank, opens):
                for c in range(4):
                    ins = mm(bank[:, c * P:(c + 1) * P], ident16[:], zero16[:], opens and c == 0,
                             not opens and c == 3)
                return ins

            def in_sbuf(l, *key):
                n = turn(l, *key)
                pe.wait_ge(free[n % RING], n // RING + 1)

            pe.wait_ge(s_setup, 9)
            pe.nop().then_inc(s_used, NBUF)
            for l in range(L):
                if l:
                    pe.wait_ge(s_xe, l * TILES)
                for i in range(TILES):
                    pe.wait_ge(s_h, 2 * l * TILES + i + 1)
                    for f in range(2):
                        transposes(l, i, "T1", f)
                for i in range(TILES):
                    for f in range(2):
                        in_sbuf(l, "T1", i, f)
                wait_piece(l, 0)
                feature_major(l, 0, 0, "ZF")
                for p, key in ((1, "CC"), (2, "CI"), (3, "CB")):
                    wait_piece(l, p)
                    for c in range(CC):
                        feature_major(l, p, c * P, key, c)
                for p0, key in ((4, "G"), (6, "V")):
                    for f in range(2):
                        wait_piece(l, p0 + f)
                        for i in range(TILES):
                            token_major(l, p0 + f, i, key, f, i)
                for p0, key in ((8, "Q"), (10, "K")):
                    for c in range(AC):
                        if c % 2 == 0:
                            wait_piece(l, p0 + c // 2)
                        feature_major(l, p0 + c // 2, c % 2 * P, key, c)
                pe.wait_ge(s_F, l + 1)
                for h in range(H):
                    b = wait_free(pe, l, "FB", h)
                    is_full(mm(b[:], ident[0:H, h:h + 1].broadcast_to([H, P]), zf[0:H, 3, :], True, True), l, "FB", h)
                pe.wait_ge(s_setup, 10 + l)
                for i in range(TILES):
                    pe.wait_ge(s_vn, l * TILES + i + 1)
                    b = wait_free(pe, l, "GM", i)
                    for g in range(GG):
                        ins = mm(b[:, g * GD:(g + 1) * GD], wsp[:, g, :], vn[:, i, g * GD:(g + 1) * GD], True, True)
                    is_full(ins, l, "GM", i)
                pe.wait_ge(s_cvsq, (l + 1) * CC)
                b = wait_free(pe, l, "CS")
                for i in range(TILES):
                    for c in range(CC):
                        ins = mm(b[:, i:i + 1], c_c[:, c, i * P:(i + 1) * P], ones[:, 0:1], c == 0, c == CC - 1)
                is_full(ins, l, "CS")
                for i in range(TILES):
                    pe.wait_ge(s_og, l * TILES + i + 1)
                    b = wait_free(pe, l, "GT", i)
                    for c in range(GC):
                        ins = nc.tensor.transpose(b[:, c * P:(c + 1) * P], ug[:, i, c * P:(c + 1) * P], ident[:])
                    is_full(ins, l, "GT", i)
                for i in range(TILES):
                    in_sbuf(l, "V", 1, i)
                for c in range(AC):
                    in_sbuf(l, "Q", c)
                    in_sbuf(l, "K", c)
                for s in range(UN + AT_LAG):
                    if s < UN:
                        i, h = s // H, s % H
                        W = (i + 1) * P
                        r = slice((h % 2) * DH, (h % 2) * DH + DH)
                        b = wait_free(pe, l, "S", s)
                        mm(b[:, 0:W], qT[r, h // 2, i * P:(i + 1) * P], kT[r, h // 2, 0:W], True, False)
                        is_full(mm(b[:, W - P:W], ident16[:], causal[:], False, True), l, "S", s)
                    if T_LAG <= s < UN + T_LAG:
                        v = s - T_LAG
                        pe.wait_ge(s_exp, l * UN + v + 1)
                        b = wait_free(pe, l, "P", v)
                        for c in range(v // H + 1):
                            ins = nc.tensor.transpose(b[:, c * P:(c + 1) * P], prob[:, v % DEEP, c * P:(c + 1) * P],
                                                      ident[:])
                        is_full(ins, l, "P", v)
                    if V_LAG <= s < UN + V_LAG:
                        w = s - V_LAG
                        i, h = w // H, w % H
                        in_sbuf(l, "P", w)
                        if w >= 2:
                            pe.wait_ge(s_oh, l * UN + w - 1)
                        for c in range(i + 1):
                            ins = mm(banks[6 + w % 2][:, 0:DH], probT[:, w % 2, c * P:(c + 1) * P],
                                     v_nat[:, c, h * DH:(h + 1) * DH], c == 0, c == i)
                        ins.then_inc(s_pv, 1)
                    if s >= AT_LAG and (s - AT_LAG) % H == H - 1:
                        i = (s - AT_LAG) // H
                        pe.wait_ge(s_oh, l * UN + (i + 1) * H)
                        b = wait_free(pe, l, "AT", i)
                        for c in range(AC):
                            ins = nc.tensor.transpose(b[:, c * P:(c + 1) * P], o_att[:, i % 2, c * P:(c + 1) * P],
                                                      ident[:])
                        is_full(ins, l, "AT", i)
                for i in range(TILES):
                    in_sbuf(l, "AT", i)
                    in_sbuf(l, "GT", i)
                for f in range(N_OUT):
                    wait_slab(pe, l, S_O + f)
                    w = slab_view(l, S_O + f)
                    for i in range(TILES):
                        for key, lo, hi in (("OA", 0, AC), ("OG", AC, AC + GC), ("OC", AC + GC, DC)):
                            b = wait_free(pe, l, key, f, i)
                            for c in range(lo, hi):
                                ins = mm(b[:], mixT[:, c, i * P:(i + 1) * P], w[:, c, :], c == lo, c == hi - 1)
                            is_full(ins, l, key, f, i)
                def activations(i):
                    pe.wait_ge(s_h, (2 * l + 1) * TILES + i + 1)
                    for f in range(2):
                        transposes(l, i, "T2", f)

                per = SLAB // P

                def first_queries(c):
                    wait_slab(pe, l, S_QY + c)
                    b = wait_free(pe, l, "QA", c)
                    w = slab_view(l, S_QY + c)
                    for u in range(per):
                        for k in range(DC):
                            ins = mm(b[:, u * P:(u + 1) * P], w[:, k, u * P:(u + 1) * P], wide[:, 0, k, :],
                                     k == 0, k == DC - 1)
                    is_full(ins, l, "QA", c)

                def first_scores(c):
                    in_sbuf(l, "QA", c)
                    b = wait_free(pe, l, "SA", c)
                    for u in range(per):
                        ins = mm(b[:, u * KEYS:(u + 1) * KEYS], qyA[:, c % 2, u * P:(u + 1) * P], keysT[:, u % 2, :],
                                 True, True)
                    is_full(ins, l, "SA", c)

                def unit_queries(c):
                    s = S_QY + 1 + c // per
                    if c % per == 0:
                        wait_slab(pe, l, s)
                    b = wait_free(pe, l, "QB", c)
                    w = slab_view(l, s)
                    for k in range(DC):
                        ins = mm(b[:, 0:TB], w[:, k, (c % per) * P:(c % per + 1) * P], wide[:, 1:TILES, k, :],
                                 k == 0, k == DC - 1)
                    is_full(ins, l, "QB", c)

                def unit_scores(c):
                    in_sbuf(l, "QB", c)
                    b = wait_free(pe, l, "SB", c)
                    for i in range(TILES - 1):
                        ins = mm(b[:, i * KEYS:(i + 1) * KEYS], qyB[c % 4][:, i * P:(i + 1) * P], keysT[:, c % 2, :],
                                 True, True)
                    is_full(ins, l, "SB", c)

                for i in range(2):
                    activations(i)
                for f in range(2):
                    in_sbuf(l, "T2", 0, f)
                first_queries(0)
                for i in range(2, TILES):
                    activations(i)
                first_scores(0)
                first_queries(1)
                for c in range(2, NQ):
                    first_queries(c)
                    first_scores(c - 1)
                for i in range(1, TILES):
                    for f in range(2):
                        in_sbuf(l, "T2", i, f)
                unit_queries(0)
                first_scores(NQ - 1)
                for c in range(1, EARLY):
                    unit_queries(c)
                    unit_scores(c - 1)
                unit_scores(EARLY - 1)
                for t in range(TILES):
                    if t >= 2:
                        pe.wait_ge(s_xe, l * TILES + t - 1)
                    if t == 1:
                        for key in order[-RING:]:
                            in_sbuf(l, *key)
                    acc = acc_banks(t)
                    for f in range(2):
                        zeros(acc[f], True)
                    for q in range(PARTS):
                        if t == 0:
                            for c in late(q):
                                unit_queries(c)
                            for c in late(q - 1):
                                unit_scores(c)
                        n0 = (l * TILES + t) * SLOTS + q * LOOP * BODY
                        with pe.Fori(0, LOOP) as it:
                            for b in range(BODY):
                                j = b % NBUF
                                pe.wait_ge(s_dg, it * BODY + (n0 + b + 1))
                                for f in range(2):
                                    ins = nc.tensor.matmul(acc[f][:], diag[:, j, :],
                                                           arena[:, j, D + f * 512:D + (f + 1) * 512],
                                                           start=False, stop=False)
                                ins.then_inc(s_used, 1)
                    for f in range(2):
                        ins = zeros(acc[f], False)
                    ins.then_inc(s_acc, 1)


def kernel(x, norm1_g, w_in, b_forget, sgu_norm_g, w_spatial, b_spatial, conv_w, mix_norm_g, w_out,
           norm2_g, w_query, sub_keys, expert_u, expert_v, final_g):
    import numpy as np
    import concourse.bacc as bacc
    from concourse.bass_utils import run_bass_kernel_spmd as run

    def chunked(w):
        l, d, n = w.shape
        return w.reshape(l, d // P, P, n).transpose(0, 2, 1, 3)

    L, D = norm1_g.shape
    arrays = {
        "x": x.reshape(-1, D),
        "norm1_g": norm1_g,
        "w_in": chunked(w_in),
        "b_forget": b_forget,
        "sgu_g": sgu_norm_g,
        "w_spatial": w_spatial.transpose(0, 3, 1, 2),
        "b_spatial": b_spatial.transpose(0, 2, 1),
        "conv_w": conv_w.reshape(L, conv_w.shape[1], -1, P).transpose(0, 3, 1, 2),
        "mix_g": mix_norm_g.reshape(L, -1, P).transpose(0, 2, 1),
        "w_out": chunked(w_out),
        "norm2_g": norm2_g,
        "w_query": chunked(w_query),
        "sub_keys": sub_keys.transpose(0, 3, 1, 2),
        "uv": np.concatenate([expert_u, expert_v], axis=2).reshape(-1, 2 * D),
        "final_g": final_g,
    }
    nc = bacc.Bacc("TRN2", target_bir_lowering=False, num_devices=1)
    fed, args = {}, []
    for name, a in arrays.items():
        a = np.ascontiguousarray(a)
        fed[f"in_{name}"] = a
        args.append(nc.dram_tensor(f"in_{name}", a.shape, mybir.dt.from_np(a.dtype), kind="ExternalInput").ap())
    out = nc.dram_tensor("out_0", arrays["x"].shape, F32, kind="ExternalOutput").ap()
    trunk_kernel(nc, *args, out)
    r = run(nc, [fed], core_ids=[0])
    return r.results[0]["out_0"].reshape(x.shape)
```
